# Optimizing a Trainium2 kernel written in Bass

```python
import jax, jax.numpy as jnp
from jax import lax
import numpy as np

D_MODEL = 2048
BATCH = 1
SEQ = 256
DEPTH = 1

HEAD_DIM = 64
NSA_WIDTH = D_MODEL // 2
NSA_HEADS = NSA_WIDTH // HEAD_DIM
NSA_KV_HEADS = NSA_HEADS // 4
NSA_KV_WIDTH = NSA_KV_HEADS * HEAD_DIM
CMP_BLOCK = 32
CMP_STRIDE = 16
CMP_HIDDEN = 4 * HEAD_DIM
SEL_BLOCK = 64
SEL_TOPK = 16
WINDOW = 512
Q_BLOCK = 128
SEL_FORCE = 1.0e4
MLSTM_WIDTH = D_MODEL // 4
MLSTM_HEADS = 4
MLSTM_HEAD_DIM = MLSTM_WIDTH // MLSTM_HEADS
MLSTM_CHUNK = 64
MLSTM_CONV = 4
CONV_CHANNELS = D_MODEL // 4
CONV_WIDTH = 31
MIX_WIDTH = NSA_WIDTH + MLSTM_WIDTH + CONV_CHANNELS
IN_SPLITS = (NSA_WIDTH, NSA_KV_WIDTH, NSA_KV_WIDTH, NSA_KV_WIDTH, NSA_KV_WIDTH, NSA_KV_WIDTH, NSA_KV_WIDTH, 3 * NSA_HEADS, MLSTM_WIDTH, MLSTM_WIDTH, MLSTM_WIDTH, MLSTM_WIDTH, MLSTM_HEADS, MLSTM_HEADS, 2 * CONV_CHANNELS)
IN_WIDTH = sum(IN_SPLITS)
N_GROUPS = 4
EXPERTS_PER_GROUP = 8
N_EXPERTS = N_GROUPS * EXPERTS_PER_GROUP
EXPERT_HIDDEN = D_MODEL // 4
TOP_K_INNER = 2
MOE_BLOCK = 128
NORM_EPS = 1e-6
LN_EPS = 1e-5

kernel_name = 'hybrid_nsa_mlstm_conformer_hmoe'

def rmsnorm(x, g):
    x32 = x.astype(jnp.float32)
    y = x32 * lax.rsqrt(jnp.mean(x32 * x32, axis=-1, keepdims=True) + NORM_EPS)
    return (y * g.astype(jnp.float32)).astype(x.dtype)

def head_rmsnorm(h, n_heads, g):
    B, S, W = h.shape
    h32 = h.astype(jnp.float32).reshape(B, S, n_heads, W // n_heads)
    h32 = h32 * lax.rsqrt(jnp.mean(h32 * h32, axis=-1, keepdims=True) + NORM_EPS)
    return (h32.reshape(B, S, W) * g.astype(jnp.float32)).astype(h.dtype)

def layernorm(x, g, b):
    x32 = x.astype(jnp.float32)
    mu = jnp.mean(x32, axis=-1, keepdims=True)
    var = jnp.mean(jnp.square(x32 - mu), axis=-1, keepdims=True)
    y = (x32 - mu) * lax.rsqrt(var + LN_EPS) * g.astype(jnp.float32) + b.astype(jnp.float32)
    return y.astype(x.dtype)

def causal_depthwise_conv(x, w, b):
    W, C = w.shape
    xp = jnp.pad(x, ((0, 0), (W - 1, 0), (0, 0)))
    y = lax.conv_general_dilated(xp, w.astype(x.dtype)[:, None, :], window_strides=(1,), padding='VALID', dimension_numbers=('NWC', 'WIO', 'NWC'), feature_group_count=C)
    return y + b.astype(x.dtype)

def masked_softmax(s, mask):
    s = jnp.where(mask, s, -jnp.inf)
    m = jnp.max(s, axis=-1, keepdims=True)
    m = jnp.where(jnp.isfinite(m), m, 0.0)
    p = jnp.exp(s - m)
    return p / jnp.maximum(jnp.sum(p, axis=-1, keepdims=True), 1e-30)

def alibi_slopes(n):
    return jnp.asarray(2.0 ** (-8.0 * np.arange(1, n + 1) / n), dtype=jnp.float32)

def selection_overlap(n_cmp, n_blk):
    cs = np.arange(n_cmp) * CMP_STRIDE
    ss = np.arange(n_blk) * SEL_BLOCK
    ov = np.minimum(cs[:, None] + CMP_BLOCK, ss[None, :] + SEL_BLOCK) - np.maximum(cs[:, None], ss[None, :])
    return jnp.asarray(np.clip(ov, 0, None) / CMP_STRIDE, dtype=jnp.float32)

def compress_blocks(x, idx, pos, w1, w2):
    blk = x[:, idx] + pos.astype(jnp.float32)[None, None, :, None, :]
    B, n, l, G, Dh = blk.shape
    blk = blk.transpose(0, 1, 3, 2, 4).reshape(B, n, G, l * Dh)
    return jax.nn.silu(blk @ w1.astype(jnp.float32)) @ w2.astype(jnp.float32)

def nsa_attention(q, k_cmp, v_cmp, k_sel, v_sel, k_win, v_win, gate_pre, cmp_pos_k, cmp_w1_k, cmp_w2_k, cmp_pos_v, cmp_w1_v, cmp_w2_v):
    f32 = jnp.float32
    B, S, _ = q.shape
    H, G, Dh = NSA_HEADS, NSA_KV_HEADS, HEAD_DIM
    HPG = H // G
    q = q.astype(f32).reshape(B, S, G, HPG, Dh) * (Dh ** -0.5)
    k_cmp, v_cmp, k_sel, v_sel, k_win, v_win = [t.astype(f32).reshape(B, S, G, Dh) for t in (k_cmp, v_cmp, k_sel, v_sel, k_win, v_win)]
    gates = jax.nn.sigmoid(gate_pre.astype(f32)).reshape(B, S, G, HPG, 3)
    slopes = alibi_slopes(H).reshape(G, HPG)[None, None, :, :, None]

    n_cmp = (S - CMP_BLOCK) // CMP_STRIDE + 1
    cmp_idx = np.arange(n_cmp)[:, None] * CMP_STRIDE + np.arange(CMP_BLOCK)[None, :]
    kc = compress_blocks(k_cmp, cmp_idx, cmp_pos_k, cmp_w1_k, cmp_w2_k)
    vc = compress_blocks(v_cmp, cmp_idx, cmp_pos_v, cmp_w1_v, cmp_w2_v)
    cmp_end = jnp.asarray(cmp_idx[:, -1], dtype=jnp.int32)

    n_blk = S // SEL_BLOCK
    n_sel = min(SEL_TOPK, n_blk)
    overlap = selection_overlap(n_cmp, n_blk)
    ksb = k_sel.reshape(B, n_blk, SEL_BLOCK, G, Dh).transpose(0, 3, 1, 2, 4)
    vsb = v_sel.reshape(B, n_blk, SEL_BLOCK, G, Dh).transpose(0, 3, 1, 2, 4)
    blk_ids = jnp.arange(n_blk)
    b_ix = jnp.arange(B)[:, None, None, None]
    g_ix = jnp.arange(G)[None, None, :, None]

    kwp = jnp.pad(k_win, ((0, 0), (WINDOW, 0), (0, 0), (0, 0)))
    vwp = jnp.pad(v_win, ((0, 0), (WINDOW, 0), (0, 0), (0, 0)))
    win_off = jnp.arange(Q_BLOCK + WINDOW)

    n_qb = S // Q_BLOCK
    q_blocks = q.reshape(B, n_qb, Q_BLOCK, G, HPG, Dh).swapaxes(0, 1)
    g_blocks = gates.reshape(B, n_qb, Q_BLOCK, G, HPG, 3).swapaxes(0, 1)

    def block_fn(args):
        qi, qb, gb = args
        t = qi * Q_BLOCK + jnp.arange(Q_BLOCK)
        d_c = t[:, None] - cmp_end[None, :]
        s_c = jnp.einsum('bqghd,bngd->bqghn', qb, kc) - slopes * d_c.astype(f32)[None, :, None, None, :]
        p_c = masked_softmax(s_c, (d_c >= 0)[None, :, None, None, :])
        o_c = jnp.einsum('bqghn,bngd->bqghd', p_c, vc)
        imp = jnp.einsum('bqgn,nj->bqgj', jnp.sum(p_c, axis=3), overlap)
        cur = t // SEL_BLOCK
        forced = (blk_ids[None, :] == 0) | (blk_ids[None, :] == cur[:, None]) | (blk_ids[None, :] == cur[:, None] - 1)
        causal_b = blk_ids[None, :] <= cur[:, None]
        imp = jnp.where(forced[None, :, None, :], SEL_FORCE, jnp.where(causal_b[None, :, None, :], imp, -SEL_FORCE))
        _, sel = lax.top_k(imp, n_sel)
        ks = ksb[b_ix, g_ix, sel].reshape(B, Q_BLOCK, G, n_sel * SEL_BLOCK, Dh)
        vs = vsb[b_ix, g_ix, sel].reshape(B, Q_BLOCK, G, n_sel * SEL_BLOCK, Dh)
        pos = (sel[..., None] * SEL_BLOCK + jnp.arange(SEL_BLOCK)).reshape(B, Q_BLOCK, G, n_sel * SEL_BLOCK)
        d_s = t[None, :, None, None] - pos
        s_s = jnp.einsum('bqghd,bqgkd->bqghk', qb, ks) - slopes * d_s.astype(f32)[:, :, :, None, :]
        p_s = masked_softmax(s_s, (d_s >= 0)[:, :, :, None, :])
        o_s = jnp.einsum('bqghk,bqgkd->bqghd', p_s, vs)
        kw = lax.dynamic_slice_in_dim(kwp, qi * Q_BLOCK, Q_BLOCK + WINDOW, axis=1)
        vw = lax.dynamic_slice_in_dim(vwp, qi * Q_BLOCK, Q_BLOCK + WINDOW, axis=1)
        kpos = qi * Q_BLOCK - WINDOW + win_off
        d_w = t[:, None] - kpos[None, :]
        m_w = (d_w >= 0) & (d_w < WINDOW) & (kpos[None, :] >= 0)
        s_w = jnp.einsum('bqghd,bkgd->bqghk', qb, kw) - slopes * d_w.astype(f32)[None, :, None, None, :]
        p_w = masked_softmax(s_w, m_w[None, :, None, None, :])
        o_w = jnp.einsum('bqghk,bkgd->bqghd', p_w, vw)
        return gb[..., 0:1] * o_c + gb[..., 1:2] * o_s + gb[..., 2:3] * o_w

    out = lax.map(block_fn, (jnp.arange(n_qb), q_blocks, g_blocks))
    return out.swapaxes(0, 1).reshape(B, S, H * Dh)

def mlstm_chunkwise(q, k, v, i_pre, f_pre):
    f32 = jnp.float32
    B, S, H, Dh = q.shape
    L = MLSTM_CHUNK
    NC = S // L

    def chunks(t):
        t = t.astype(f32).reshape((B, NC, L, H) + t.shape[3:])
        return jnp.moveaxis(t, 3, 1)

    qc, kc, vc = chunks(q), chunks(k) * (Dh ** -0.5), chunks(v)
    ig = chunks(i_pre)
    b = jnp.cumsum(jax.nn.log_sigmoid(chunks(f_pre)), axis=-1)
    b_end = b[..., -1]
    a = b_end[..., None] - b + ig
    a_max = jnp.max(a, axis=-1)
    w = jnp.exp(a - a_max[..., None])
    C_chunk = jnp.einsum('bhcsk,bhcsv->bhckv', kc * w[..., None], vc)
    n_chunk = jnp.einsum('bhcs,bhcsk->bhck', w, kc)

    def step(carry, inp):
        C, n, m = carry
        be, am, Cc, nc = inp
        m_new = jnp.maximum(be + m, am)
        sp = jnp.exp(be + m - m_new)
        sc = jnp.exp(am - m_new)
        return (sp[..., None, None] * C + sc[..., None, None] * Cc, sp[..., None] * n + sc[..., None] * nc, m_new), (C, n, m)

    init = (jnp.zeros((B, H, Dh, Dh), f32), jnp.zeros((B, H, Dh), f32), jnp.zeros((B, H), f32))
    xs = (jnp.moveaxis(b_end, 2, 0), jnp.moveaxis(a_max, 2, 0), jnp.moveaxis(C_chunk, 2, 0), jnp.moveaxis(n_chunk, 2, 0))
    _, (C0, n0, m0) = lax.scan(step, init, xs)
    C0 = jnp.moveaxis(C0, 0, 2)
    n0 = jnp.moveaxis(n0, 0, 2)
    m0 = jnp.moveaxis(m0, 0, 2)

    causal = jnp.tril(jnp.ones((L, L), dtype=bool))
    D = jnp.where(causal, b[..., :, None] - b[..., None, :] + ig[..., None, :], -jnp.inf)
    inter = b + m0[..., None]
    m_t = jnp.maximum(inter, jnp.max(D, axis=-1))
    s = jnp.einsum('bhctd,bhcsd->bhcts', qc, kc) * jnp.exp(D - m_t[..., None])
    w_inter = jnp.exp(inter - m_t)
    num = jnp.einsum('bhcts,bhcsd->bhctd', s, vc) + w_inter[..., None] * jnp.einsum('bhctk,bhckv->bhctv', qc, C0)
    den = jnp.sum(s, axis=-1) + w_inter * jnp.einsum('bhctk,bhck->bhct', qc, n0)
    h = num / jnp.maximum(jnp.abs(den), jnp.exp(-m_t))[..., None]
    return jnp.moveaxis(h, 1, 3).reshape(B, S, H, Dh)

def hybrid_mixer(h, w_in, cmp_pos_k, cmp_w1_k, cmp_w2_k, cmp_pos_v, cmp_w1_v, cmp_w2_v, nsa_out_g, mlstm_conv_w, mlstm_conv_b, mlstm_i_bias, mlstm_f_bias, mlstm_out_g, conv_w, conv_b, conv_ln_g, conv_ln_b, w_out):
    B, S, _ = h.shape
    points = [int(p) for p in np.cumsum(IN_SPLITS)[:-1]]
    (q, k_c, v_c, k_s, v_s, k_w, v_w, g_nsa, mq, mk, mv, mo, mi, mf, cu) = jnp.split(h @ w_in, points, axis=-1)
    a_out = nsa_attention(q, k_c, v_c, k_s, v_s, k_w, v_w, g_nsa, cmp_pos_k, cmp_w1_k, cmp_w2_k, cmp_pos_v, cmp_w1_v, cmp_w2_v)
    a_out = head_rmsnorm(a_out.astype(h.dtype), NSA_HEADS, nsa_out_g)
    qk = jax.nn.silu(causal_depthwise_conv(jnp.concatenate([mq, mk], axis=-1), mlstm_conv_w, mlstm_conv_b))
    mq, mk = jnp.split(qk, 2, axis=-1)
    shp = (B, S, MLSTM_HEADS, MLSTM_HEAD_DIM)
    hm = mlstm_chunkwise(mq.reshape(shp), mk.reshape(shp), mv.reshape(shp), mi + mlstm_i_bias, mf + mlstm_f_bias)
    hm = (jax.nn.sigmoid(mo.astype(jnp.float32)) * hm.reshape(B, S, MLSTM_WIDTH)).astype(h.dtype)
    hm = head_rmsnorm(hm, MLSTM_HEADS, mlstm_out_g)
    ca, cg = jnp.split(cu, 2, axis=-1)
    c = causal_depthwise_conv(ca * jax.nn.sigmoid(cg), conv_w, conv_b)
    c = jax.nn.silu(layernorm(c, conv_ln_g, conv_ln_b))
    return jnp.concatenate([a_out, hm, c], axis=-1) @ w_out

def hier_moe(xn, router_w_group, router_b_group, router_w_expert, router_b_expert, w_gate, w_up, w_down):
    f32 = jnp.float32
    B, S, D = xn.shape
    T = B * S
    x2 = xn.reshape(T, D)
    pg = jax.nn.softmax((x2 @ router_w_group).astype(f32) + router_b_group.astype(f32), axis=-1)
    pg_top, grp = lax.top_k(pg, 1)
    le = (x2 @ router_w_expert).astype(f32).reshape(T, N_GROUPS, EXPERTS_PER_GROUP) + router_b_expert.astype(f32)
    le = jnp.take_along_axis(le, jnp.broadcast_to(grp[:, :, None], (T, 1, EXPERTS_PER_GROUP)), axis=1)[:, 0]
    pe_top, e_local = lax.top_k(jax.nn.softmax(le, axis=-1), TOP_K_INNER)
    gate = pg_top * pe_top / jnp.sum(pe_top, axis=-1, keepdims=True)
    expert = grp * EXPERTS_PER_GROUP + e_local
    flat_e = expert.reshape(-1)
    flat_w = gate.reshape(-1)
    flat_tok = jnp.repeat(jnp.arange(T, dtype=jnp.int32), TOP_K_INNER)
    A = flat_e.shape[0]
    order = jnp.argsort(flat_e)
    e_sorted = flat_e[order]
    counts = jnp.bincount(flat_e, length=N_EXPERTS)
    starts = jnp.cumsum(counts) - counts
    padded = (counts + MOE_BLOCK - 1) // MOE_BLOCK * MOE_BLOCK
    pends = jnp.cumsum(padded)
    dest = (pends - padded)[e_sorted] + jnp.arange(A) - starts[e_sorted]
    n_blocks = (A + MOE_BLOCK - 1) // MOE_BLOCK + N_EXPERTS
    P = n_blocks * MOE_BLOCK
    row_tok = jnp.zeros((P,), jnp.int32).at[dest].set(flat_tok[order])
    row_w = jnp.zeros((P,), f32).at[dest].set(flat_w[order])
    blk_e = jnp.minimum(jnp.searchsorted(pends, jnp.arange(n_blocks) * MOE_BLOCK, side='right'), N_EXPERTS - 1)

    def block_fn(args):
        tok, wt, e = args
        xb = x2[tok]
        hb = jax.nn.silu(xb @ w_gate[e]) * (xb @ w_up[e])
        return (hb @ w_down[e]) * wt[:, None].astype(xb.dtype)

    yb = lax.map(block_fn, (row_tok.reshape(n_blocks, MOE_BLOCK), row_w.reshape(n_blocks, MOE_BLOCK), blk_e))
    y = jnp.zeros((T, D), x2.dtype).at[row_tok].add(yb.reshape(P, D))
    return y.reshape(B, S, D)

def setup_inputs(seed: int = 0) -> dict:
    key = jax.random.key(seed)
    ks = jax.random.split(key, 40)
    f32 = jnp.float32
    L, D = DEPTH, D_MODEL

    def nrm(k, shape, scale):
        return jax.random.normal(k, shape, f32) * scale

    def gain(k, shape):
        return 1.0 + 0.02 * jax.random.normal(k, shape, f32)

    return {
        'x': nrm(ks[0], (BATCH, SEQ, D), 1.0),
        'attn_norm_g': gain(ks[1], (L, D)),
        'w_in': nrm(ks[2], (L, D, IN_WIDTH), D ** -0.5),
        'cmp_pos_k': nrm(ks[3], (L, CMP_BLOCK, HEAD_DIM), 0.1),
        'cmp_w1_k': nrm(ks[4], (L, CMP_BLOCK * HEAD_DIM, CMP_HIDDEN), (CMP_BLOCK * HEAD_DIM) ** -0.5),
        'cmp_w2_k': nrm(ks[5], (L, CMP_HIDDEN, HEAD_DIM), CMP_HIDDEN ** -0.5),
        'cmp_pos_v': nrm(ks[6], (L, CMP_BLOCK, HEAD_DIM), 0.1),
        'cmp_w1_v': nrm(ks[7], (L, CMP_BLOCK * HEAD_DIM, CMP_HIDDEN), (CMP_BLOCK * HEAD_DIM) ** -0.5),
        'cmp_w2_v': nrm(ks[8], (L, CMP_HIDDEN, HEAD_DIM), CMP_HIDDEN ** -0.5),
        'nsa_out_g': gain(ks[9], (L, NSA_WIDTH)),
        'mlstm_conv_w': nrm(ks[10], (L, MLSTM_CONV, 2 * MLSTM_WIDTH), MLSTM_CONV ** -0.5),
        'mlstm_conv_b': nrm(ks[11], (L, 2 * MLSTM_WIDTH), 0.01),
        'mlstm_i_bias': nrm(ks[12], (L, MLSTM_HEADS), 0.1),
        'mlstm_f_bias': 3.0 + 3.0 * jax.random.uniform(ks[13], (L, MLSTM_HEADS), f32),
        'mlstm_out_g': gain(ks[14], (L, MLSTM_WIDTH)),
        'conv_w': nrm(ks[15], (L, CONV_WIDTH, CONV_CHANNELS), CONV_WIDTH ** -0.5),
        'conv_b': nrm(ks[16], (L, CONV_CHANNELS), 0.01),
        'conv_ln_g': gain(ks[17], (L, CONV_CHANNELS)),
        'conv_ln_b': nrm(ks[18], (L, CONV_CHANNELS), 0.01),
        'w_out': nrm(ks[19], (L, MIX_WIDTH, D), MIX_WIDTH ** -0.5),
        'ffn_norm_g': gain(ks[20], (L, D)),
        'router_w_group': nrm(ks[21], (L, D, N_GROUPS), D ** -0.5),
        'router_b_group': nrm(ks[22], (L, N_GROUPS), 0.01),
        'router_w_expert': nrm(ks[23], (L, D, N_EXPERTS), D ** -0.5),
        'router_b_expert': nrm(ks[24], (L, N_GROUPS, EXPERTS_PER_GROUP), 0.01),
        'expert_w_gate': nrm(ks[25], (L, N_EXPERTS, D, EXPERT_HIDDEN), D ** -0.5),
        'expert_w_up': nrm(ks[26], (L, N_EXPERTS, D, EXPERT_HIDDEN), D ** -0.5),
        'expert_w_down': nrm(ks[27], (L, N_EXPERTS, EXPERT_HIDDEN, D), EXPERT_HIDDEN ** -0.5),
        'final_norm_g': gain(ks[28], (D,)),
    }

def reference(x, attn_norm_g, w_in, cmp_pos_k, cmp_w1_k, cmp_w2_k, cmp_pos_v, cmp_w1_v, cmp_w2_v, nsa_out_g, mlstm_conv_w, mlstm_conv_b, mlstm_i_bias, mlstm_f_bias, mlstm_out_g, conv_w, conv_b, conv_ln_g, conv_ln_b, w_out, ffn_norm_g, router_w_group, router_b_group, router_w_expert, router_b_expert, expert_w_gate, expert_w_up, expert_w_down, final_norm_g):
    for l in range(DEPTH):
        h = rmsnorm(x, attn_norm_g[l])
        x = x + hybrid_mixer(h, w_in[l], cmp_pos_k[l], cmp_w1_k[l], cmp_w2_k[l], cmp_pos_v[l], cmp_w1_v[l], cmp_w2_v[l], nsa_out_g[l], mlstm_conv_w[l], mlstm_conv_b[l], mlstm_i_bias[l], mlstm_f_bias[l], mlstm_out_g[l], conv_w[l], conv_b[l], conv_ln_g[l], conv_ln_b[l], w_out[l])
        h = rmsnorm(x, ffn_norm_g[l])
        x = x + hier_moe(h, router_w_group[l], router_b_group[l], router_w_expert[l], router_b_expert[l], expert_w_gate[l], expert_w_up[l], expert_w_down[l])
    return rmsnorm(x, final_norm_g)


_drawn_inputs = setup_inputs


def setup_inputs(seed=0):
    import zlib

    import numpy as np

    out = dict(_drawn_inputs(seed))
    spreads = {}
    factors = {'cmp_pos_k': 8.0,
     'nsa_out_g': 3.447,
     'mlstm_conv_b': 7.356,
     'mlstm_i_bias': 200.0,
     'mlstm_out_g': 5.582,
     'conv_b': 8.0,
     'conv_ln_g': 5.652,
     'conv_ln_b': 6.081,
     'ffn_norm_g': 3.307,
     'router_b_group': 4.209,
     'router_b_expert': 8.0,
     'final_norm_g': 20.456}
    for name, (base, spread) in spreads.items():
        noise = np.random.default_rng([zlib.crc32(name.encode()), seed]).standard_normal(out[name].shape)
        drawn = base * np.exp(spread * noise) if base else spread * noise
        out[name] = __import__('jax').numpy.asarray(drawn.astype(out[name].dtype))
    for name, factor in factors.items():
        out[name] = (out[name] * factor).astype(out[name].dtype)
    return out
```

```python
from contextlib import ExitStack

import concourse.bass as bass
import numpy as np
from concourse import mybir

F32 = mybir.dt.float32
I32 = mybir.dt.int32
ALU = mybir.AluOpType
ACT = mybir.ActivationFunctionType
AX = mybir.AxisListType.X

P = 128
T = 256
TT = T // P
D = 2048
DK = D // P
DH = 64
HEADS, GROUPS, HPG = 16, 4, 4
CMP_N, CMP_J = 15, 16
ML_H, ML_D = 4, 128
CT = 4
TAPS, ML_TAPS = 31, 4
EPS, LN_EPS = 1e-6, 1e-5
NEG = -1.0e30
E, EG, EI = 32, 4, 8
SLOTS = 64
RING = 6
QUAD = 4
NQUAD = E // QUAD
CHUNKS = 6
ROUNDS = T // SLOTS
PAR_DMAS = 14
ROUTER_DMAS = 10
OV_PE, OV_ACT, OV_DVE = 16, 13, 5

WIDTH = dict(q=1024, kc=256, vc=256, ks=256, vs=256, kw=256, vw=256, gate=48, mq=512, mk=512, mv=512, mo=512,
             mi=4, mf=4, ca=512, cg=512)
COL = dict(zip(WIDTH, np.cumsum([0] + list(WIDTH.values()))[:-1].tolist()))
SMALL = WIDTH["gate"] + WIDTH["mi"] + WIDTH["mf"]

SLABS = ["cg0", "cg1", "ca0", "ca1", "mq0", "mq1", "mk0", "mk1", "small", "mv0", "mv1", "mo0", "mo1",
         "kc0", "vc0", "ks0", "kw0", "w1k", "w1v", "vs0", "q0", "q1", "q2", "q3", "vw0"]


def projection_units():
    units = []
    for n, name in enumerate(SLABS):
        part, s = (name, 0) if name in ("small", "w1k", "w1v") else (name[:-1], int(name[-1]))
        if part in ("small", "mv", "mo", "vs", "vw"):
            units += [(n, part, "rows", s, t) for t in range(TT)]
        elif part in ("w1k", "w1v"):
            units.append((n, part, "hidden", 0, 0))
        elif part == "q":
            if s % 2:
                units += [(n, part, "heads", s // 2, i) for i in range(HPG)]
        else:
            units += [(n, part, "columns", s, i) for i in range(2)]
    return units


UNITS = projection_units()


def units_through(slab):
    if SLABS[slab] in ("q0", "q2"):
        slab += 1
    return max(u for u, unit in enumerate(UNITS) if unit[0] == slab) + 1


def units_before(part):
    return min(u for u, unit in enumerate(UNITS) if unit[1] == part)


def units_with(part):
    return max(u for u, unit in enumerate(UNITS) if unit[1] == part) + 1


OUT_SLOTS = [2, 4, 0, 2]
OUT_DMAS = 5
CHUNK_SLOT = [(c + 4) % RING for c in range(CHUNKS)]
CHUNK_DMAS = [2, 2, 2, 2, 1, 1]
CHUNK_INC = [16 * n for n in CHUNK_DMAS]

PAR = {}
_at = 0
for _name, _n in (("attn_g", 16), ("nsa_g", 8), ("ml_g", 4), ("mconv_w", 32), ("mconv_b", 8), ("conv_b", 4),
                  ("ln_g", 4), ("ln_b", 4), ("pos_k", 16), ("pos_v", 16)):
    PAR[_name] = _at
    _at += _n
PAR_ROWS = _at
TAP_ROWS = TAPS * CT

KEYS = 16 + 2 * 256
ATT = [(p, g, t) for p in range(2) for t in range(TT) for g in range(2)]
SLOPES = [2.0 ** (-8.0 * (h + 1) / HEADS) for h in range(HEADS)]


def build(nc, x, attn_norm_g, w_in, cmp_pos_k, cmp_w1_k, cmp_w2_k, cmp_pos_v, cmp_w1_v, cmp_w2_v, nsa_out_g,
          mlstm_conv_w, mlstm_conv_b, mlstm_i_bias, mlstm_f_bias, mlstm_out_g, conv_w, conv_b, conv_ln_g,
          conv_ln_b, w_out, ffn_norm_g, router_w_group, router_b_group, router_w_expert, router_b_expert,
          expert_w_gate, expert_w_up, expert_w_down, final_norm_g, out):
    with ExitStack() as ctx:
        def sb(name, shape, dt=F32, stack=ctx):
            return stack.enter_context(nc.sbuf_tensor(name, shape, dt))

        def sem(name):
            return ctx.enter_context(nc.semaphore(name))

        PS = ctx.enter_context(nc.psum_tensor("PS", [P, 8, 512], F32))

        ring = sb("ring", [P, RING, DK, 256])
        x1 = sb("x1", [P, TT, D])
        ident = sb("ident", [P, P])
        ones = sb("ones", [P, P])
        upto = sb("upto", [P, P])
        before = sb("before", [P, P])
        small_c = sb("small_c", [P, 8])
        EPS_C, LN_EPS_C, ONE_C, ZERO_C = (small_c[:, i:i + 1] for i in range(4))
        st = sb("st", [P, 16])
        countdown = sb("countdown", [P, E])
        slot_id = sb("slot_id", [P, SLOTS])
        rout_b = sb("rout_b", [P, EG + E])
        roww = sb("roww", [P, DK, EG + E])

        mixer = ExitStack()

        def mb(name, shape, dt=F32):
            return sb(name, shape, dt, mixer)

        mix = mb("mix", [P, DK, T])
        hn = mix[:, :, :].rearrange("p a b -> p (a b)").rearrange("p (t d) -> p t d", t=TT)
        mqk = mix[:, 0:8, :]
        cgs = mix[:, 8:12, :]
        cacc = mix[:, 12:16, :]
        hT = mb("hT", [P, DK, T])
        nsa_q = mb("nsa_q", [P, 8, T])
        tmp = nsa_q[:, 0:4, :]
        diag = nsa_q[:, 4:8, :].rearrange("p a b -> p (a b)").rearrange("p (t n) -> p t n", t=TT)
        keys = mb("keys", [P, 2, KEYS])
        vals = mb("vals", [P, 2, TT, 256])
        gates = mb("gates", [P, TT, SMALL])
        fi_b = mb("fi_b", [P, 8])
        par = mb("par", [P, PAR_ROWS])
        taps = mb("taps", [P, TAP_ROWS])
        vcs = mb("vcs", [32, GROUPS, DH])
        w2 = mb("w2", [P, 2, 2, DH])
        cmask = mb("cmask", [P, P])
        dist = mb("dist", [P, 2, P])
        dist_c = mb("dist_c", [P, TT, 16])
        av_ln = vals[:, 1, 1, 0:P]
        av_hd = mb("av_hd", [P, P])
        ml = mb("ml", [P, 12, TT, ML_H])
        gmb = mb("gmb", [P, ML_H, 3, P])
        prow, trow = gmb[:, 0, 0, :], gmb[:, 0, 1, :]
        kcv = gmb[:, :, :, :].rearrange("p a b c -> p (a b c)")[:, 0:1024].rearrange("p (a b) -> p a b", a=4)
        mv = mb("mv", [P, TT, 512])
        mo = mb("mo", [P, TT, 512])
        pT = mb("pT", [P, 2, 512])
        hid = mb("hid", [P, 512])
        att = mb("att", [P, 4096])
        cin = att[:, 0:CT * 286].rearrange("p (c t) -> p c t", c=CT)
        m_in = att[:, 1152:1152 + 8 * 259].rearrange("p (c t) -> p c t", c=8)
        blk = att[:, 1152:1152 + 2 * CMP_J * 60].rearrange("p (b j n) -> p b j n", b=2, j=CMP_J)
        sc = att[:, :].rearrange("p (u h b k) -> p u h b k", u=2, h=HPG, b=2)
        osq = att[:, 0:2048]
        oroot_b = att[:, 2048:4096]
        sc_c = mb("sc_c", [P, 2, HPG, 16])
        rs = mb("rs", [P, 2, 3, HPG, 3])
        mixer.close()

        xn = sb("xn", [P, TT, DK, P])
        XG = sb("XG", [P, DK, QUAD * SLOTS])
        Y2 = sb("Y2", [P, 2, D])
        sel = sb("sel", [P, TT, QUAD, SLOTS])
        selw = sb("selw", [P, TT, QUAD, SLOTS])
        SW = sb("SW", [P, 2, T])
        Hs = sb("Hs", [P, 512])
        sg = sb("sg", [P, 4, SLOTS])
        hTe = sb("hTe", [P, 4, SLOTS])
        fin_g = sb("fin_g", [P, D])
        ro = sb("ro", [P, 12, TT, E])
        rt = sb("rt", [P, 16, TT])
        rank = sb("rank", [P, TT, E + QUAD])
        wgt = sb("wgt", [P, TT, E + QUAD])
        cnt = sb("cnt", [1, E], I32)
        xnT = XG
        ffn_g = Y2[:, 0, :]

        x_loaded = sem("x_loaded")
        par_loaded = sem("par_loaded")
        small_loaded = sem("small_loaded")
        w2_loaded = sem("w2_loaded")
        bias_loaded = sem("bias_loaded")
        router_loaded = sem("router_loaded")
        gain_loaded = sem("gain_loaded")
        fing_loaded = sem("fing_loaded")
        w_loaded = [sem(f"w_loaded{s}") for s in range(RING)]
        const_step = sem("const_step")
        consts_ready = sem("consts_ready")
        ssq_ready = sem("ssq_ready")
        rstd_root = sem("rstd_root")
        hn_ready = sem("hn_ready")
        par_turned = sem("par_turned")
        par_ready = sem("par_ready")
        h_turned = sem("h_turned")
        hT_ready = sem("hT_ready")
        unit_done = sem("unit_done")
        unit_saved = sem("unit_saved")
        pads_ready = sem("pads_ready")
        conv_gated = sem("conv_gated")
        conv_step = sem("conv_step")
        ln_sum = sem("ln_sum")
        ln_sq = sem("ln_sq")
        ln_cen = sem("ln_cen")
        ln_root = sem("ln_root")
        ln_done = sem("ln_done")
        conv_out = sem("conv_out")
        mconv_step = sem("mconv_step")
        mconv_out = sem("mconv_out")
        dve_step = sem("dve_step")
        act_step = sem("act_step")
        lf_ready = sem("lf_ready")
        lf_exp = sem("lf_exp")
        lf_log = sem("lf_log")
        f_in = sem("f_in")
        f_summed = sem("f_summed")
        diag_ready = sem("diag_ready")
        g_spread = sem("g_spread")
        gm_ready = sem("gm_ready")
        decay_ready = sem("decay_ready")
        qk_done = sem("qk_done")
        s_ready = sem("s_ready")
        s_turned = sem("s_turned")
        sT_ready = sem("sT_ready")
        num_done = sem("num_done")
        hm_ready = sem("hm_ready")
        hm_sq = sem("hm_sq")
        hm_root = sem("hm_root")
        hm_norm = sem("hm_norm")
        hm_turned = sem("hm_turned")
        hm_out = sem("hm_out")
        blk_ready = sem("blk_ready")
        hid_turned = sem("hid_turned")
        hidT_ready = sem("hidT_ready")
        cmp_done = sem("cmp_done")
        cmp_saved = sem("cmp_saved")
        scored = sem("scored")
        biased = sem("biased")
        max_ready = sem("max_ready")
        exp_done = sem("exp_done")
        p_ready = sem("p_ready")
        p_turned = sem("p_turned")
        pT_ready = sem("pT_ready")
        pv_done = sem("pv_done")
        o_saved = sem("o_saved")
        osq_ready = sem("osq_ready")
        oms_done = sem("oms_done")
        oroot = sem("oroot")
        o_normed = sem("o_normed")
        attn_out = sem("attn_out")
        out_done = sem("out_done")
        out_added = sem("out_added")
        ffn_ssq = sem("ffn_ssq")
        ffn_root = sem("ffn_root")
        xn_ready = sem("xn_ready")
        xn_turned = sem("xn_turned")
        xnT_ready = sem("xnT_ready")
        logits_done = sem("logits_done")
        route_max = sem("route_max")
        route_exp = sem("route_exp")
        picks_ready = sem("picks_ready")
        ranks_done = sem("ranks_done")
        counts_ready = sem("counts_ready")
        zeroed = sem("zeroed")
        sel_made = sem("sel_made")
        sel_ready = sem("sel_ready")
        g_filled = sem("g_filled")
        g_saved = sem("g_saved")
        w_used = [sem(f"w_used{c}") for c in range(CHUNKS)]
        h_saved = sem("h_saved")
        h_turned_e = sem("h_turned_e")
        silu_done = sem("silu_done")
        hid_ready = sem("hid_ready")
        y_saved_a = sem("y_saved_a")
        y_saved_d = sem("y_saved_d")
        sw_filled = sem("sw_filled")
        sw_saved = sem("sw_saved")
        sc_filled = sem("sc_filled")
        sc_added = sem("sc_added")
        ov_loaded = sem("ov_loaded")
        ov_step = sem("ov_step")
        ov_sel = sem("ov_sel")
        ov_pe = sem("ov_pe")
        ov_act = sem("ov_act")
        ov_dve = sem("ov_dve")
        ov_end = sem("ov_end")
        ov_left = sem("ov_left")
        fin_ssq = sem("fin_ssq")
        fin_root = sem("fin_root")
        fin_ready = sem("fin_ready")
        stored = sem("stored")

        block = ctx.enter_context(nc.Block())

        w_in_v = w_in[0].rearrange("(k p) n -> p k n", p=P)
        w1_v = {"w1k": cmp_w1_k[0].rearrange("(k p) n -> p k n", p=P),
                "w1v": cmp_w1_v[0].rearrange("(k p) n -> p k n", p=P)}
        wo_heads = w_out[0, 0:1024, :].rearrange("(p g i d) n -> p g d i n", p=2, g=2, i=HPG)
        wo_rest = w_out[0, 1024:2048, :].rearrange("(k p) n -> p k n", p=P)
        ring_out = [ring[:, s:s + 2, :, :].rearrange("p a k n -> p (a k n)").rearrange("p (k n) -> p k n", k=DK)
                    for s in range(RING - 1)]
        ring_flat = ring[:, :, :, :].rearrange("p s k n -> p s (k n)")
        gate_v = expert_w_gate[0].rearrange("e (c p j) n -> e c p (j n)", c=4, j=4)
        up_v = expert_w_up[0].rearrange("e (c p j) n -> e c p (j n)", c=4, j=4)
        down_v = expert_w_down[0].rearrange("e (c j p) n -> e c p j n", c=2, j=2)

        def chunk_parts(e, c):
            dst = ring_flat[:, CHUNK_SLOT[c], :]
            pick = slice(e, e + 1) if isinstance(e, int) else e
            if c < 4:
                return [(dst[:, 0:2048], gate_v[pick, c].rearrange("e p n -> (e p) n")),
                        (dst[:, 2048:4096], up_v[pick, c].rearrange("e p n -> (e p) n"))]
            return [(dst.rearrange("p (j n) -> p j n", j=2), down_v[pick, c - 4].rearrange("e p j n -> (e p) j n"))]

        def rows_of(dram, n):
            return dram.rearrange("(r c) -> r c", r=n)

        slot_total = [0] * RING
        slab_at = []
        for n in range(len(SLABS)):
            slot_total[n % RING] += 16
            slab_at.append(slot_total[n % RING])
        out_at = []
        for s in OUT_SLOTS:
            slot_total[s] += 16 * OUT_DMAS
            out_at.append(slot_total[s])

        @block.sync
        def _(sp):
            for t in range(TT):
                sp.dma_start(x1[:, t, :], x[0, t * P:(t + 1) * P, :]).then_inc(x_loaded, 16)
            for n, name in enumerate(SLABS):
                if n >= RING:
                    sp.wait_ge(unit_done, units_through(n - RING))
                dst = ring[:, n % RING, :, :]
                if name == "small":
                    gate = COL["gate"]
                    ig = COL["mi"]
                    sp.dma_start(dst[:, :, 0:48], w_in_v[:, :, gate:gate + 48]).then_inc(small_loaded, 16)
                    sp.dma_start(dst[:, :, 48:56], w_in_v[:, :, ig:ig + 8]).then_inc(w_loaded[n % RING], 16)
                elif name in w1_v:
                    sp.dma_start(dst, w1_v[name]).then_inc(w_loaded[n % RING], 16)
                else:
                    c = COL[name[:-1]] + 256 * int(name[-1])
                    sp.dma_start(dst, w_in_v[:, :, c:c + 256]).then_inc(w_loaded[n % RING], 16)
            last_use = {n % RING: units_through(n) for n in range(len(SLABS))}
            for m, s in enumerate(OUT_SLOTS):
                if m < 3:
                    sp.wait_ge(unit_done, max(last_use[s], last_use[s + 1]))
                else:
                    sp.wait_ge(out_done, TT)
                cols = slice(512 * m, 512 * m + 512)
                for p in range(2):
                    for g in range(2):
                        sp.dma_start(ring_out[s][64 * g:64 * g + 64, 4 * p:4 * p + 4, :],
                                     wo_heads[p, g, :, :, cols]).then_inc(w_loaded[s], 16)
                sp.dma_start(ring_out[s][:, 8:16, :], wo_rest[:, :, cols]).then_inc(w_loaded[s], 16)

            def load_chunk(e, c, done, by=16):
                for dst, src in chunk_parts(e, c):
                    sp.dma_start(dst, src).then_inc(done, by)

            for c in range(CHUNKS):
                sp.wait_ge(out_done, TT * [2, 2, 3, 3, 4, 4][c])
                load_chunk(0, c, w_loaded[CHUNK_SLOT[c]])
            looped = (E - 1) // QUAD
            with sp.Fori(0, looped) as q:
                for i in range(1, QUAD + 1):
                    for c in range(CHUNKS):
                        sp.wait_ge(w_used[c], q * QUAD + i)
                        load_chunk(bass.ds(q * QUAD + i, 1), c, w_loaded[CHUNK_SLOT[c]])
            for e in range(looped * QUAD + 1, E):
                for c in range(CHUNKS):
                    sp.wait_ge(w_used[c], e)
                    load_chunk(e, c, w_loaded[CHUNK_SLOT[c]])

            sp.wait_ge(counts_ready, 2)
            with sp.Fori(0, E) as e:
                n = sp.value_load(cnt[0:1, bass.ds(e, 1)], min_val=0, max_val=T)
                with sp.If(n > SLOTS):
                    for c in range(CHUNKS):
                        if c == 0:
                            sp.wait_ge(w_used[CHUNKS - 1], E)
                        load_chunk(bass.ds(e, 1), c, ov_loaded)
                    sp.wait_ge(ov_end, e + 1)
                    sp.sem_inc(ov_left, 1)
                with sp.Else():
                    sp.sem_inc(ov_loaded, sum(CHUNK_INC))
            for t in range(TT):
                sp.wait_ge(fin_ready, t + 1)
                sp.dma_start(out[0, t * P:(t + 1) * P, :], x1[:, t, :]).then_inc(stored, 16)
            sp.wait_ge(stored, 16 * TT)

        @block.gpsimd
        def _(pool):
            done = [0]

            def step(ins):
                done[0] += 1
                ins.then_inc(const_step, 1)
                pool.wait_ge(const_step, done[0])

            def triangle(tile, base, fill, col, row, op=ALU.is_ge):
                step(pool.affine_select(out=tile, in_=tile, compare_op=op, fill=fill, base=base,
                                        pattern=[[col, tile.shape[1]]], channel_multiplier=row))

            step(pool.memset(ident[:, :], 0.0))
            triangle(ident[:, :], 0, 1.0, -1, 1, ALU.not_equal)
            step(pool.memset(ones[:, :], 1.0))
            for i, v in enumerate((EPS, LN_EPS, 1.0, 0.0)):
                step(pool.memset(small_c[:, i:i + 1], v))
            pool.memset(hid[:, :], 0.0).then_inc(consts_ready, 1)
            step(pool.memset(upto[:, :], 1.0))
            triangle(upto[:, :], 0, 0.0, 1, -1)
            step(pool.memset(before[:, :], 1.0))
            triangle(before[:, :], -1, 0.0, 1, -1)
            step(pool.memset(cmask[:, :], 0.0))
            triangle(cmask[:, :], 0, NEG, -1, 1)
            for i in range(2):
                step(pool.iota(dist[:, i, :], [[1, P]], base=-P * (1 - i), channel_multiplier=-1,
                               allow_small_or_imprecise_dtypes=True))
            triangle(dist[:, 1, :], 0, NEG, -1, 1)
            for t in range(TT):
                step(pool.iota(dist_c[:, t, :], [[16, 16]], base=31 - P * t, channel_multiplier=-1,
                               allow_small_or_imprecise_dtypes=True))
                triangle(dist_c[:, t, :], P * t - 31, NEG, -16, 1)
            step(pool.memset(dist_c[:, :, CMP_N:16], NEG))
            step(pool.memset(av_ln, 1.0 / (CT * P)))
            step(pool.memset(av_hd[:, :], 0.0))
            for h in (0, 64):
                step(pool.memset(av_hd[h:h + 64, h:h + 64], 1.0 / DH))
            step(pool.iota(countdown[:, :], [[-1, E]], base=E, channel_multiplier=0,
                           allow_small_or_imprecise_dtypes=True))
            step(pool.iota(slot_id[:, :], [[1, SLOTS]], base=0, channel_multiplier=0,
                           allow_small_or_imprecise_dtypes=True))
            step(pool.memset(keys[:, :, CMP_N:16], 0.0))
            step(pool.memset(cin[:, :, 0:TAPS - 1], 0.0))
            pool.memset(m_in[:, :, 0:ML_TAPS - 1], 0.0).then_inc(consts_ready, 1)

        @block.tensor
        def _(pe):
            pe.wait_ge(consts_ready, 1)
            pe.wait_ge(par_loaded, 16 * PAR_DMAS)
            pe.transpose(PS[:, 0, 0:PAR_ROWS], prow[0:PAR_ROWS, :], ident[0:PAR_ROWS, 0:PAR_ROWS])
            pe.transpose(PS[:, 1, 0:TAP_ROWS], trow[0:TAP_ROWS, :], ident[0:TAP_ROWS, 0:TAP_ROWS])\
                .then_inc(par_turned, 1)
            for f in range(8):
                if f >= 4:
                    pe.wait_ge(hT_ready, 2 * (f - 3))
                for k in (2 * f, 2 * f + 1):
                    for t in range(TT):
                        pe.wait_ge(hn_ready, t + 1)
                        mm = pe.transpose(PS[:, 4 + f % 4, (k % 2) * T + t * P:(k % 2) * T + (t + 1) * P],
                                          hn[:, t, k * P:(k + 1) * P], ident[:, :])
                mm.then_inc(h_turned, 1)

            def forget_sum():
                pe.wait_ge(lf_ready, 1)
                pe.wait_ge(consts_ready, 2)
                pe.matmul(PS[:, 4, 0:4], upto[:, :], ml[:, 3, 0, :], start=True, stop=True)
                pe.matmul(PS[:, 4, 4:8], ones[:, :], ml[:, 3, 0, :], start=True, stop=False)
                pe.matmul(PS[:, 4, 4:8], upto[:, :], ml[:, 3, 1, :], start=False, stop=True).then_inc(f_summed, 1)

            def ln_mean():
                pe.wait_ge(conv_step, TAPS * CT)
                for c in range(CT):
                    mm = pe.matmul(PS[:, 5, 0:T], av_ln, cacc[:, c, :], start=(c == 0), stop=(c == CT - 1))
                mm.then_inc(ln_sum, 1)

            def ln_square():
                pe.wait_ge(ln_cen, 1)
                for c in range(CT):
                    mm = pe.matmul(PS[:, 6, 0:T], av_ln, tmp[:, c, :], start=(c == 0), stop=(c == CT - 1))
                mm.then_inc(ln_sq, 1)

            def spread_gates():
                pe.wait_ge(diag_ready, 1)
                for t, b in ((0, 4), (1, 7)):
                    mm = pe.matmul(PS[:, b, :], ones[:, :], diag[:, t, :], start=True, stop=True)
                mm.then_inc(g_spread, 1)

            def mlstm_scores():
                pe.wait_ge(mconv_out, 1)
                pe.wait_ge(gm_ready, 1)
                pe.wait_ge(ln_done, 1)
                for h in range(ML_H):
                    pe.matmul(PS[:, 4 + h, 0:P], mqk[:, h, 0:P], mqk[:, 4 + h, 0:P], start=True, stop=True)
                    pe.matmul(PS[:, 4 + h, P:3 * P], mqk[:, h, P:T], mqk[:, 4 + h, :], start=True, stop=True)\
                        .then_inc(qk_done, 1)

            def mlstm_turn():
                for h in range(ML_H):
                    pe.wait_ge(s_ready, h + 1)
                    for i in range(3):
                        mm = pe.transpose(PS[:, 4 + h, i * P:(i + 1) * P], gmb[:, h, i, :], ident[:, :])
                    mm.then_inc(s_turned, 1)

            def mlstm_values():
                for h in range(ML_H):
                    pe.wait_ge(sT_ready, h + 1)
                    s, v = pT[:, h % 2, :], slice(h * ML_D, (h + 1) * ML_D)
                    pe.matmul(PS[:, 4 + h, 0:P], s[:, 0:P], mv[:, 0, v], start=True, stop=True)
                    pe.matmul(PS[:, 4 + h, P:T], s[:, P:2 * P], mv[:, 0, v], start=True, stop=False)
                    pe.matmul(PS[:, 4 + h, P:T], s[:, 2 * P:3 * P], mv[:, 1, v], start=False, stop=True)\
                        .then_inc(num_done, 1)

            def mlstm_columns():
                pe.wait_ge(hm_norm, 1)
                for h in range(ML_H):
                    for t in range(TT):
                        mm = pe.transpose(PS[:, 4 + h, t * P:(t + 1) * P], mo[:, t, h * ML_D:(h + 1) * ML_D],
                                          ident[:, :])
                    mm.then_inc(hm_turned, 1)

            def hidden_columns():
                pe.wait_ge(unit_saved, units_with("w1v"))
                pe.wait_ge(hm_out, ML_H)
                for k in range(2):
                    mm = pe.transpose(PS[:, 4, k * P:(k + 1) * P], hid[:, k * P:(k + 1) * P], ident[:, :])
                mm.then_inc(hid_turned, 1)

            def compressed():
                pe.wait_ge(hidT_ready, 1)
                pe.wait_ge(w2_loaded, 32)
                hT2 = hid[:, 256:512].rearrange("p (k n) -> p k n", k=2)
                for half in (0, 64):
                    for k in range(2):
                        pe.matmul(PS[half:half + 64, 5, 0:60], w2[:, 0, k, :], hT2[:, k, 0:60],
                                  start=(k == 0), stop=(k == 1))
                for g in range(GROUPS):
                    for k in range(2):
                        mm = pe.matmul(PS[0:CMP_N, 6, g * DH:(g + 1) * DH],
                                       hT2[:, k, 64 + g * CMP_N:64 + (g + 1) * CMP_N], w2[:, 1, k, :],
                                       start=(k == 0), stop=(k == 1))
                mm.then_inc(cmp_done, 1)

            between = {25: [forget_sum, ln_mean], 27: [ln_square], 29: [spread_gates], 31: [mlstm_scores],
                       33: [mlstm_turn, mlstm_values], 37: [mlstm_columns], 41: [hidden_columns],
                       45: [compressed]}
            pe.wait_ge(hT_ready, DK)
            for u, (n, part, kind, s, i) in enumerate(UNITS):
                pe.wait_ge(w_loaded[n % RING], slab_at[n])
                if part == "small":
                    pe.wait_ge(small_loaded, 16)
                if part == "q":
                    pe.wait_ge(w_loaded[(n - 1) % RING], slab_at[n - 1])
                if kind == "hidden":
                    pe.wait_ge(blk_ready, 1)
                if u >= 4:
                    pe.wait_ge(unit_saved, u - 3)
                w = ring[:, n % RING, :, :]
                b = PS[:, u % 4, :]
                for k in range(DK):
                    if kind == "rows":
                        cols = SMALL if part == "small" else 256
                        dst, lhs, rhs = b[:, 0:cols], hT[:, k, i * P:(i + 1) * P], w[:, k, 0:cols]
                    elif kind == "heads":
                        for g in range(2):
                            mm = pe.matmul(b[64 * g:64 * g + 64, 0:T],
                                           ring[:, n % RING - 1 + g, k, i * DH:(i + 1) * DH], hT[:, k, :],
                                           start=(k == 0), stop=(k == DK - 1))
                        continue
                    elif kind == "hidden":
                        r = 64 * (part == "w1v")
                        dst, lhs, rhs = b[r:r + 60, 0:256], blk[:, r // 64, k, :], w[:, k, :]
                    else:
                        dst, lhs, rhs = b[:, 0:T], w[:, k, i * P:(i + 1) * P], hT[:, k, :]
                    mm = pe.matmul(dst, lhs, rhs, start=(k == 0), stop=(k == DK - 1))
                mm.then_inc(unit_done, 1)
                for piece in between.get(u, []):
                    piece()

            pe.wait_ge(unit_saved, len(UNITS))
            pe.wait_ge(cmp_saved, 1)
            tile, turn = [0], [0]

            def scores(a):
                p, g, t = ATT[a]
                rows = slice(64 * g, 64 * g + 64)
                for i in range(HPG):
                    for c0, c1 in ((0, 272), (272, 528))[:t + 1]:
                        if tile[0] >= 4:
                            pe.wait_ge(biased, tile[0] - 3)
                        pe.matmul(PS[:, tile[0] % 4, 0:c1 - c0], nsa_q[rows, 4 * p + i, t * P:(t + 1) * P],
                                  keys[rows, p, c0:c1], start=True, stop=True).then_inc(scored, 1)
                        tile[0] += 1

            def attend(a):
                p, g, t = ATT[a]
                G = 2 * p + g
                steps = [(0, k) for k in range(t + 1)] + [(1, k) for k in range(t + 1)] + [(2, 0)]
                o = PS[64 * g:64 * g + 64, 6 + a % 2, :]
                m0 = turn[0]
                pe.wait_ge(p_ready, a + 1)

                def turned(j):
                    br, k = steps[j]
                    m = m0 + j
                    if m >= 2:
                        pe.wait_ge(pT_ready, m - 1)
                    for i in range(HPG):
                        if br < 2:
                            mm = pe.transpose(PS[:, 4 + m % 2, i * P:(i + 1) * P],
                                              sc[:, a % 2, i, br, k * P:(k + 1) * P], ident[:, :])
                        else:
                            mm = pe.transpose(PS[0:16, 4 + m % 2, i * P:(i + 1) * P], sc_c[:, a % 2, i, :],
                                              ident[:, :])
                    mm.then_inc(p_turned, 1)

                turned(0)
                for j, (br, k) in enumerate(steps):
                    if j + 1 < len(steps):
                        turned(j + 1)
                    m = m0 + j
                    pe.wait_ge(pT_ready, m + 1)
                    if j == 0 and a >= 2:
                        pe.wait_ge(o_saved, a - 1)
                    lhs = vals[:, br, k, G * DH:(G + 1) * DH] if br < 2 else vcs[0:CMP_N, G, :]
                    rhs = pT[:, m % 2, :] if br < 2 else pT[0:CMP_N, m % 2, :]
                    pe.matmul(o, lhs, rhs, start=(j == 0), stop=(br == 2)).then_inc(pv_done, 1)
                turn[0] += len(steps)

            scores(0)
            for a in range(len(ATT)):
                if a + 1 < len(ATT):
                    scores(a + 1)
                attend(a)
            for c in range(4):
                pe.wait_ge(osq_ready, c + 1)
                pe.matmul(PS[:, c, :], av_hd[:, :], osq[:, c * 512:(c + 1) * 512], start=True, stop=True)\
                    .then_inc(oms_done, 1)

            pe.wait_ge(conv_out, CT)
            for m, s in enumerate(OUT_SLOTS):
                pe.wait_ge(w_loaded[s], out_at[m])
                for t in range(TT):
                    v = TT * m + t
                    if v >= 4:
                        pe.wait_ge(out_added, v - 3)
                    elif v == 0:
                        pe.wait_ge(o_saved, len(ATT))
                    order = list(range(8, DK)) + list(range(8))
                    for j, k in enumerate(order):
                        if v == 0 and k < 8:
                            pe.wait_ge(attn_out, k + 1)
                        mm = pe.matmul(PS[:, 4 + v % 4, :], mix[:, k, t * P:(t + 1) * P], ring_out[s][:, k, :],
                                       start=(j == 0), stop=(j == DK - 1))
                    mm.then_inc(out_done, 1)

            pe.wait_ge(router_loaded, 16 * ROUTER_DMAS)
            for f in range(8):
                if f >= 4:
                    pe.wait_ge(xnT_ready, f - 3)
                for k in (2 * f, 2 * f + 1):
                    for t in range(TT):
                        pe.wait_ge(xn_ready, t + 1)
                        mm = pe.transpose(PS[:, f % 4, (k % 2) * T + t * P:(k % 2) * T + (t + 1) * P],
                                          xn[:, t, k, :], ident[:, :])
                mm.then_inc(xn_turned, 1)
            pe.wait_ge(xnT_ready, 8)
            pe.wait_ge(out_added, 2 * TT * 2)
            for t in range(TT):
                for k in range(DK):
                    mm = pe.matmul(PS[:, 4, t * 64:t * 64 + EG + E], xnT[:, k, t * P:(t + 1) * P], roww[:, k, :],
                                   start=(k == 0), stop=(k == DK - 1))
            mm.then_inc(logits_done, 1)
            pe.wait_ge(picks_ready, 1)
            A = ro[:, 0, :, :]
            pe.matmul(PS[:, 5, 0:E], before[:, :], A[:, 0, :], start=True, stop=True)
            pe.matmul(PS[:, 5, 64:64 + E], ones[:, :], A[:, 0, :], start=True, stop=False)
            pe.matmul(PS[:, 5, 64:64 + E], before[:, :], A[:, 1, :], start=False, stop=True)
            pe.matmul(PS[0:1, 6, 0:E], ones[:, 0:1], A[:, 0, :], start=True, stop=False)
            pe.matmul(PS[0:1, 6, 0:E], ones[:, 0:1], A[:, 1, :], start=False, stop=True).then_inc(ranks_done, 1)

            def gather(n, w0, width, saved0):
                for f in range(8):
                    if f >= 2:
                        pe.wait_ge(n, saved0 + (f - 1))
                    for k in (2 * f, 2 * f + 1):
                        for t in range(TT):
                            mm = pe.matmul(PS[:, 6 + f % 2, (k % 2) * 256:(k % 2) * 256 + width],
                                           xn[:, t, k, :], sel[:, t, :, :].rearrange("p a b -> p (a b)")[:, 0:width],
                                           start=(t == 0), stop=(t == TT - 1))
                    mm.then_inc(g_filled, 1)

            def gate_up(i, c):
                w = ring_flat[:, CHUNK_SLOT[c], :].rearrange("p (u j n) -> p u j n", u=2, j=4)
                for j in range(4):
                    for u in range(2):
                        mm = pe.matmul(PS[64 * u:64 * u + 64, 0, :], XG[:, 4 * c + j, i * SLOTS:(i + 1) * SLOTS],
                                       w[:, u, j, :], start=(c == 0 and j == 0), stop=(c == 3 and j == 3))
                return mm

            def hidden_turn():
                for k in range(4):
                    mm = pe.transpose(PS[:, 1, k * P:(k + 1) * P], Hs[:, k * P:(k + 1) * P], ident[:, :])
                return mm

            def down(c):
                w = ring_flat[:, CHUNK_SLOT[c], :].rearrange("p (j n) -> p j n", j=2)
                for j in range(2):
                    k = 2 * (c - 4) + j
                    for b in range(2):
                        for half in range(2):
                            mm = pe.matmul(PS[64 * half:64 * half + 64, 2 + b, :], hTe[:, k, :],
                                           w[:, j, half * 1024 + b * 512:half * 1024 + (b + 1) * 512],
                                           start=(k == 0), stop=(k == 3))
                return mm

            def scatter(pair, t, cols, rows=P):
                for b in range(2):
                    mm = pe.matmul(PS[:, 4 + b, :], SW[0:rows, pair, t * P:(t + 1) * P],
                                   Y2[0:rows, pair, (2 * cols + b) * 512:(2 * cols + b + 1) * 512],
                                   start=True, stop=True)
                mm.then_inc(sc_filled, 1)

            def turn_weights(rows, pairs):
                for pair in range(pairs):
                    for t in range(TT):
                        mm = pe.transpose(
                            PS[0:rows, 6, pair * T + t * P:pair * T + (t + 1) * P],
                            selw[:, t, :, :].rearrange("p a b -> p (a b)")[:, pair * P:pair * P + rows], ident[:, :])
                mm.then_inc(sw_filled, 1)

            pe.wait_ge(zeroed, 1)
            pe.wait_ge(counts_ready, 2)
            with pe.Fori(0, NQUAD) as q:
                pe.wait_ge(sel_ready, q + 1)
                gather(g_saved, 0, QUAD * SLOTS, q * 8)
                pe.wait_ge(g_saved, q * 8 + 8)
                for i in range(QUAD):
                    for c in range(4):
                        pe.wait_ge(w_loaded[CHUNK_SLOT[c]],
                                   q * (QUAD * CHUNK_INC[c]) + ((i + 1) * CHUNK_INC[c] + slot_total[CHUNK_SLOT[c]]))
                        gate_up(i, c).then_inc(w_used[c], 1)
                    pair, t = (i // 2 + 1) % 2, i % 2
                    if t == 0:
                        pe.wait_ge(y_saved_a, q * QUAD + (i + 1))
                        pe.wait_ge(y_saved_d, q * QUAD + (i + 1))
                    pe.wait_ge(sc_added, q * 8 + (2 * i + 1))
                    scatter(pair, t, 0)
                    pe.wait_ge(h_saved, q * QUAD + (i + 1))
                    hidden_turn().then_inc(h_turned_e, 1)
                    pe.wait_ge(sc_added, q * 8 + (2 * i + 2))
                    scatter(pair, t, 1)
                    pe.wait_ge(hid_ready, q * QUAD + (i + 2))
                    pe.wait_ge(y_saved_a, q * QUAD + (i + 1))
                    pe.wait_ge(y_saved_d, q * QUAD + (i + 1))
                    for c in range(4, 6):
                        pe.wait_ge(w_loaded[CHUNK_SLOT[c]],
                                   q * (QUAD * CHUNK_INC[c]) + ((i + 1) * CHUNK_INC[c] + slot_total[CHUNK_SLOT[c]]))
                        down(c).then_inc(w_used[c], 1)
                    if i == 1:
                        turn_weights(P, 2)
                        pe.wait_ge(sw_saved, q + 1)
            pe.wait_ge(y_saved_a, E + 1)
            pe.wait_ge(y_saved_d, E + 1)
            for t in range(TT):
                for cols in range(2):
                    pe.wait_ge(sc_added, 8 * NQUAD + 2 * t + cols + 1)
                    scatter(1, t, cols)

            with pe.Fori(0, E) as e:
                n = pe.value_load(cnt[0:1, bass.ds(e, 1)], min_val=0, max_val=T)
                with pe.If(n > SLOTS):
                    with pe.Fori(0, ROUNDS - 1) as r:
                        at = e * (ROUNDS - 1) + r
                        pe.wait_ge(ov_sel, at + 1)
                        for f in range(8):
                            if f >= 2:
                                pe.wait_ge(ov_act, at * OV_ACT + (f - 1))
                            for k in (2 * f, 2 * f + 1):
                                for t in range(TT):
                                    mm = pe.matmul(PS[:, 6 + f % 2, (k % 2) * 256:(k % 2) * 256 + SLOTS],
                                                   xn[:, t, k, :], sel[:, t, 0, :], start=(t == 0), stop=(t == TT - 1))
                            mm.then_inc(ov_pe, 1)
                        pe.wait_ge(ov_act, at * OV_ACT + 8)
                        pe.wait_ge(ov_loaded, e * sum(CHUNK_INC) + sum(CHUNK_INC))
                        for c in range(4):
                            mm = gate_up(0, c)
                        mm.then_inc(ov_pe, 1)
                        pe.wait_ge(ov_act, at * OV_ACT + 9)
                        hidden_turn().then_inc(ov_pe, 1)
                        pe.wait_ge(ov_dve, at * OV_DVE + 1)
                        for c in range(4, 6):
                            mm = down(c)
                        mm.then_inc(ov_pe, 1)
                        for t in range(TT):
                            mm = pe.transpose(PS[0:SLOTS, 6, t * P:(t + 1) * P], selw[:, t, 0, :], ident[:, :])
                        mm.then_inc(ov_pe, 1)
                        pe.wait_ge(ov_act, at * OV_ACT + 13)
                        for t in range(TT):
                            for cols in range(2):
                                pe.wait_ge(ov_dve, at * OV_DVE + (1 + 2 * t + cols))
                                for b in range(2):
                                    mm = pe.matmul(PS[:, 4 + b, :], SW[0:SLOTS, 0, t * P:(t + 1) * P],
                                                   Y2[0:SLOTS, 0, (2 * cols + b) * 512:(2 * cols + b + 1) * 512],
                                                   start=True, stop=True)
                                mm.then_inc(ov_pe, 1)
                    pe.wait_ge(ov_end, e + 1)
                    pe.sem_inc(ov_left, 1)
                with pe.Else():
                    pe.sem_inc(ov_pe, (ROUNDS - 1) * OV_PE)

        @block.scalar
        def _(act):
            def load_rows(dst, src, done=par_loaded):
                act.dma_start(dst, src).then_inc(done, 16)

            def at(name, n):
                return prow[PAR[name]:PAR[name] + n, :]

            load_rows(at("attn_g", 16), attn_norm_g[0].rearrange("(r c) -> r c", c=P))
            heads_g = nsa_out_g[0].rearrange("(p g i d) -> p g i d", p=2, g=2, i=HPG)
            for p in range(2):
                for g in range(2):
                    r = PAR["nsa_g"] + 4 * p
                    load_rows(prow[r:r + 4, 64 * g:64 * g + 64], heads_g[p, g])
            load_rows(at("ml_g", 4), mlstm_out_g[0].rearrange("(r c) -> r c", c=P))
            load_rows(at("mconv_w", 32), mlstm_conv_w[0].rearrange("k (r c) -> (k r) c", c=P))
            load_rows(at("mconv_b", 8), mlstm_conv_b[0].rearrange("(r c) -> r c", c=P))
            load_rows(at("conv_b", 4), conv_b[0].rearrange("(r c) -> r c", c=P))
            load_rows(at("ln_g", 4), conv_ln_g[0].rearrange("(r c) -> r c", c=P))
            load_rows(at("ln_b", 4), conv_ln_b[0].rearrange("(r c) -> r c", c=P))
            load_rows(at("pos_k", 16), cmp_pos_k[0].rearrange("(r l) d -> r (l d)", l=2))
            load_rows(at("pos_v", 16), cmp_pos_v[0].rearrange("(r l) d -> r (l d)", l=2))
            load_rows(trow[0:TAP_ROWS, :], conv_w[0].rearrange("k (r c) -> (k r) c", c=P))

            act_n = [0]

            def step(ins):
                act_n[0] += 1
                ins.then_inc(act_step, 1)
                act.wait_ge(act_step, act_n[0])

            act.wait_ge(consts_ready, 1)
            act.wait_ge(x_loaded, 16 * TT)
            for t in range(TT):
                step(act.activation(hn[:, t, :], x1[:, t, :], ACT.Square, bias=ZERO_C, accum_out=st[:, t:t + 1]))
            act.activation(st[:, 2:4], st[:, 0:2], ACT.Sqrt, bias=EPS_C, scale=1.0 / D).then_inc(rstd_root, 1)
            load_rows(w2[:, 0, :, :], cmp_w2_k[0].rearrange("(k p) n -> p k n", p=P), w2_loaded)
            load_rows(w2[:, 1, :, :], cmp_w2_v[0].rearrange("(k p) n -> p k n", p=P), w2_loaded)
            load_rows(fi_b[:, 0:4], mlstm_i_bias[0].partition_broadcast(P), bias_loaded)
            load_rows(fi_b[:, 4:8], mlstm_f_bias[0].partition_broadcast(P), bias_loaded)
            load_rows(rout_b[:, 0:EG], router_b_group[0].partition_broadcast(P), router_loaded)
            load_rows(rout_b[:, EG:EG + E], router_b_expert[0].rearrange("g e -> (g e)").partition_broadcast(P),
                      router_loaded)
            rg = router_w_group[0].rearrange("(c p j) n -> c p j n", c=4, j=4)
            re = router_w_expert[0].rearrange("(c p j) n -> c p j n", c=4, j=4)
            for c in range(4):
                load_rows(roww[:, 4 * c:4 * c + 4, 0:EG], rg[c], router_loaded)
                load_rows(roww[:, 4 * c:4 * c + 4, EG:EG + E], re[c], router_loaded)

            def conv_silu():
                act.wait_ge(mconv_step, 8 * ML_TAPS)
                act.activation(mqk, mqk, ACT.Silu, bias=ZERO_C).then_inc(mconv_out, 1)

            def forget_logs():
                act.wait_ge(f_in, 1)
                act.activation(ml[:, 1, :, :], ml[:, 0, :, :], ACT.Exp, bias=ZERO_C).then_inc(lf_exp, 1)
                act.wait_ge(lf_exp, 1)
                act.activation(ml[:, 2, :, :], ml[:, 1, :, :], ACT.Ln, bias=ONE_C).then_inc(lf_log, 1)

            def ln_std():
                act.wait_ge(ln_sq, 1)
                act.activation(pT[:, 0, 0:T], PS[:, 6, 0:T], ACT.Sqrt, bias=LN_EPS_C).then_inc(ln_root, 1)

            def conv_result():
                act.wait_ge(ln_done, 1)
                for c in range(CT):
                    act.activation(cacc[:, c, :], cacc[:, c, :], ACT.Silu, bias=par[:, PAR["ln_b"] + c:PAR["ln_b"] + c + 1],
                                   scale=par[:, PAR["ln_g"] + c:PAR["ln_g"] + c + 1]).then_inc(conv_out, 1)

            def decays():
                act.wait_ge(gm_ready, 1)
                for h in range(ML_H):
                    act.activation(gmb[:, h, 0, :], gmb[:, h, 0, :], ACT.Exp, bias=ml[:, 7, 0, h:h + 1])\
                        .then_inc(decay_ready, 1)
                    act.activation(gmb[:, h, 1:3, :], gmb[:, h, 1:3, :], ACT.Exp, bias=ml[:, 7, 1, h:h + 1])\
                        .then_inc(decay_ready, 1)
                act.activation(ml[:, 8, :, :], ml[:, 9, :, :], ACT.Exp, bias=ZERO_C).then_inc(decay_ready, 1)

            def mlstm_saves():
                for h in range(ML_H):
                    act.wait_ge(s_turned, h + 1)
                    if h >= 2:
                        act.wait_ge(num_done, h - 1)
                    act.activation(pT[:, h % 2, 0:3 * P], PS[:, 4 + h, 0:3 * P], ACT.Copy).then_inc(sT_ready, 1)

            def mlstm_root():
                act.wait_ge(hm_sq, 1)
                act.activation(ml[:, 11, :, :], ml[:, 10, :, :], ACT.Sqrt, bias=EPS_C, scale=1.0 / ML_D)\
                    .then_inc(hm_root, 1)

            def mlstm_result():
                for h in range(ML_H):
                    act.wait_ge(hm_turned, h + 1)
                    act.activation(mix[:, 8 + h, :], PS[:, 4 + h, 0:T], ACT.Copy,
                                   scale=par[:, PAR["ml_g"] + h:PAR["ml_g"] + h + 1]).then_inc(hm_out, 1)

            def hidden_save():
                act.wait_ge(hid_turned, 1)
                act.activation(hid[:, 256:512], PS[:, 4, 0:256], ACT.Copy).then_inc(hidT_ready, 1)

            def compressed_save():
                act.wait_ge(cmp_done, 1)
                for half in range(2):
                    src = PS[64 * half:64 * half + 64, 5, 0:60].rearrange("d (p g n) -> d p g n", p=2, g=2)
                    step(act.activation(keys[64 * half:64 * half + 64, :, 0:CMP_N], src[:, :, half, :], ACT.Copy))
                act.activation(vcs[0:CMP_N, :, :], PS[0:CMP_N, 6, 0:256].rearrange("n (g d) -> n g d", g=GROUPS),
                               ACT.Copy).then_inc(cmp_saved, 1)

            between = {19: [conv_silu], 21: [forget_logs], 27: [ln_std], 29: [conv_result], 31: [decays],
                       33: [mlstm_saves], 35: [mlstm_root], 37: [mlstm_result], 41: [hidden_save],
                       45: [compressed_save]}

            def save_unit(u):
                n, part, kind, s, i = UNITS[u]
                b = PS[:, u % 4, 0:256]
                f, scale, c = ACT.Copy, 1.0, 2 * s + i
                if part == "cg":
                    dst, f = cgs[:, c, :], ACT.Sigmoid
                elif part == "ca":
                    dst = cin[:, c, TAPS - 1:]
                elif part in ("mq", "mk"):
                    dst = m_in[:, c + 4 * (part == "mk"), ML_TAPS - 1:]
                elif part == "small":
                    b = b[:, 0:SMALL]
                    step(act.activation(gates[:, i, 0:48], b[:, 0:48], ACT.Sigmoid, bias=ZERO_C))
                    return act.activation(gates[:, i, 48:56], b[:, 48:56], ACT.Copy)
                elif part == "mv":
                    dst = mv[:, i, s * 256:(s + 1) * 256]
                elif part == "mo":
                    dst, f = mo[:, i, s * 256:(s + 1) * 256], ACT.Sigmoid
                elif part in ("kc", "vc"):
                    dst = kcv[:, i + 2 * (part == "vc"), :]
                elif part in ("ks", "kw"):
                    c0 = 16 + P * (part == "kw")
                    dst = keys[:, i, c0:c0 + 384].rearrange("d (t k) -> d t k", k=P)[:, ::2, :]
                    b = b.rearrange("d (t k) -> d t k", t=TT)
                elif part in ("vs", "vw"):
                    dst = vals[:, int(part == "vw"), i, :]
                elif part == "q":
                    dst, scale = nsa_q[:, 4 * s + i, :], DH ** -0.5
                else:
                    r = 64 * (part == "w1v")
                    dst, b, f = hid[r:r + 60, 0:256], b[r:r + 60], ACT.Silu
                if f == ACT.Copy:
                    return act.activation(dst, b, f, scale=scale)
                return act.activation(dst, b, f, bias=ZERO_C[0:b.shape[0]] if part != "w1v" else small_c[64:124, 3:4])

            for u in range(len(UNITS)):
                if u == units_before("q"):
                    act.wait_ge(g_spread, 1)
                act.wait_ge(unit_done, u + 1)
                save_unit(u).then_inc(unit_saved, 1)
                for piece in between.get(u, []):
                    piece()
            act.wait_ge(unit_done, len(UNITS))
            load_rows(fin_g[:, :], ffn_norm_g[0].partition_broadcast(P), gain_loaded)

            turn = [0]

            def exponents(a):
                p, g, t = ATT[a]
                act.wait_ge(max_ready, a + 1)
                u, w = a % 2, P * (t + 1)
                for i in range(HPG):
                    for br in range(2):
                        s = sc[:, u, i, br, 0:w]
                        act.activation(s, s, ACT.Exp, bias=rs[:, u, 0, i, 1 + br:2 + br],
                                       accum_out=rs[:, u, 1, i, 1 + br:2 + br])
                    s = sc_c[:, u, i, :]
                    e = act.activation(s, s, ACT.Exp, bias=rs[:, u, 0, i, 0:1], accum_out=rs[:, u, 1, i, 0:1])
                e.then_inc(exp_done, 1)

            def attend_saves(a):
                p, g, t = ATT[a]
                n = 2 * (t + 1) + 1
                for j in range(n):
                    m = turn[0] + j
                    act.wait_ge(p_turned, m + 1)
                    if m >= 2:
                        act.wait_ge(pv_done, m - 1)
                    rows = P if j < n - 1 else 16
                    act.activation(pT[0:rows, m % 2, :], PS[0:rows, 4 + m % 2, :], ACT.Copy).then_inc(pT_ready, 1)
                turn[0] += n
                act.wait_ge(pv_done, turn[0])
                rows = slice(64 * g, 64 * g + 64)
                act.activation(mix[rows, 4 * p:4 * p + 4, t * P:(t + 1) * P],
                               PS[rows, 6 + a % 2, :].rearrange("d (i q) -> d i q", i=HPG), ACT.Copy)\
                    .then_inc(o_saved, 1)

            exponents(0)
            for a in range(len(ATT)):
                if a + 1 < len(ATT):
                    exponents(a + 1)
                attend_saves(a)
            for c in range(4):
                act.wait_ge(oms_done, c + 1)
                act.activation(oroot_b[:, c * 512:(c + 1) * 512], PS[:, c, :], ACT.Sqrt, bias=EPS_C)\
                    .then_inc(oroot, 1)

            act.wait_ge(out_added, TT * 4)
            for t in range(TT):
                step(act.activation(xn[:, t, :, :].rearrange("p k n -> p (k n)"), x1[:, t, :], ACT.Square,
                                    bias=ZERO_C, accum_out=st[:, 6 + t:7 + t]))
            act.activation(st[:, 8:10], st[:, 6:8], ACT.Sqrt, bias=EPS_C, scale=1.0 / D).then_inc(ffn_root, 1)
            for f in range(8):
                act.wait_ge(xn_turned, f + 1)
                act.activation(xnT[:, 2 * f:2 * f + 2, :], PS[:, f % 4, :].rearrange("p (k n) -> p k n", k=2),
                               ACT.Copy).then_inc(xnT_ready, 1)
            act.wait_ge(route_max, 1)
            act.activation(rt[:, 10, :], rt[:, 9, :], ACT.Exp, bias=ZERO_C).then_inc(route_exp, 1)
            act.activation(ro[:, 7, :, 0:EG], ro[:, 6, :, 0:EG], ACT.Exp, bias=ZERO_C).then_inc(route_exp, 1)
            act.wait_ge(xn_ready, TT)
            load_rows(fin_g[:, :], final_norm_g.partition_broadcast(P), fing_loaded)

            def save_gather(f, width):
                act.activation(XG[:, 2 * f:2 * f + 2, 0:width],
                               PS[:, 6 + f % 2, :].rearrange("p (k n) -> p k n", k=2)[:, :, 0:width],
                               ACT.Copy).then_inc(g_saved if width > SLOTS else ov_act, 1)

            HT = PS[:, 1, :].rearrange("p (k n) -> p k n", k=4)
            act.wait_ge(counts_ready, 2)
            act.sem_inc(y_saved_a, 1)
            with act.Fori(0, NQUAD) as q:
                for f in range(8):
                    act.wait_ge(g_filled, q * 8 + (f + 1))
                    save_gather(f, QUAD * SLOTS)
                for i in range(QUAD):
                    act.wait_ge(w_used[3], q * QUAD + (i + 1))
                    act.activation(Hs[:, :], PS[:, 0, :], ACT.Copy).then_inc(h_saved, 1)
                    act.wait_ge(h_turned_e, q * QUAD + (i + 1))
                    act.wait_ge(hid_ready, q * QUAD + (i + 1))
                    act.activation(sg[:, :, :], HT[:, :, 0:SLOTS], ACT.Silu, bias=ZERO_C).then_inc(silu_done, 1)
                    act.wait_ge(w_used[5], q * QUAD + (i + 1))
                    r = 64 * (i % 2)
                    act.activation(Y2[r:r + 64, i // 2, 0:1024],
                                   PS[0:64, 2:4, :].rearrange("p a b -> p (a b)"), ACT.Copy).then_inc(y_saved_a, 1)
                    if i == 1:
                        act.wait_ge(sw_filled, q + 1)
                        act.activation(SW[:, :, :], PS[:, 6, :].rearrange("p (a b) -> p a b", a=2), ACT.Copy)\
                            .then_inc(sw_saved, 1)

            with act.Fori(0, E) as e:
                n = act.value_load(cnt[0:1, bass.ds(e, 1)], min_val=0, max_val=T)
                with act.If(n > SLOTS):
                    with act.Fori(0, ROUNDS - 1) as r:
                        at0 = e * (ROUNDS - 1) + r
                        for f in range(8):
                            act.wait_ge(ov_pe, at0 * OV_PE + (f + 1))
                            save_gather(f, SLOTS)
                        act.wait_ge(ov_pe, at0 * OV_PE + 9)
                        act.activation(Hs[:, :], PS[:, 0, :], ACT.Copy).then_inc(ov_act, 1)
                        act.wait_ge(ov_pe, at0 * OV_PE + 10)
                        act.activation(sg[:, :, :], HT[:, :, 0:SLOTS], ACT.Silu, bias=ZERO_C).then_inc(ov_act, 1)
                        act.wait_ge(ov_pe, at0 * OV_PE + 11)
                        for half in range(2):
                            act.activation(Y2[0:64, 0, 1024 * half:1024 * (half + 1)],
                                           PS[64 * half:64 * half + 64, 2:4, :].rearrange("p a b -> p (a b)"),
                                           ACT.Copy).then_inc(ov_act, 1)
                        act.wait_ge(ov_pe, at0 * OV_PE + 12)
                        act.activation(SW[0:64, 0, :], PS[0:64, 6, 0:T], ACT.Copy).then_inc(ov_act, 1)
                    act.wait_ge(ov_end, e + 1)
                    act.sem_inc(ov_left, 1)
                with act.Else():
                    act.sem_inc(ov_act, (ROUNDS - 1) * OV_ACT)
            act.wait_ge(ov_end, E)
            for t in range(TT):
                step(act.activation(Y2[:, t, :], x1[:, t, :], ACT.Square, bias=ZERO_C,
                                    accum_out=st[:, 10 + t:11 + t]))
            act.activation(st[:, 12:14], st[:, 10:12], ACT.Sqrt, bias=EPS_C, scale=1.0 / D).then_inc(fin_root, 1)

        @block.vector
        def _(dve):
            dve_n = [0]

            def step(ins):
                dve_n[0] += 1
                ins.then_inc(dve_step, 1)
                dve.wait_ge(dve_step, dve_n[0])

            def col(name, i):
                return par[:, PAR[name] + i:PAR[name] + i + 1]

            dve.wait_ge(par_turned, 1)
            step(dve.tensor_copy(par[:, :], PS[:, 0, 0:PAR_ROWS]))
            step(dve.tensor_copy(taps[:, :], PS[:, 1, 0:TAP_ROWS]))
            dve.wait_ge(rstd_root, 1)
            step(dve.reciprocal(st[:, 4:6], st[:, 2:4]))
            for t in range(TT):
                dve.tensor_scalar(hn[:, t, :], x1[:, t, :], st[:, 4 + t:5 + t], None, ALU.mult).then_inc(hn_ready, 1)
            for k in range(DK):
                dve.wait_ge(h_turned, k // 2 + 1)
                dve.tensor_scalar(hT[:, k, :], PS[:, 4 + (k // 2) % 4, (k % 2) * T:(k % 2 + 1) * T],
                                  col("attn_g", k), None, ALU.mult).then_inc(hT_ready, 1)

            dve.wait_ge(unit_saved, units_with("ca"))
            dve.wait_ge(consts_ready, 2)
            step(dve.tensor_tensor(cin[:, :, TAPS - 1:], cin[:, :, TAPS - 1:], cgs, ALU.mult))
            for j in range(TAPS):
                for c in range(CT):
                    src, w = cin[:, c, j:j + T], taps[:, j * CT + c:j * CT + c + 1]
                    if j == 0:
                        ins = dve.tensor_scalar(cacc[:, c, :], src, w, col("conv_b", c), ALU.mult, ALU.add)
                    else:
                        dve.wait_ge(conv_step, CT * (j - 1) + c + 1)
                        ins = dve.scalar_tensor_tensor(out=cacc[:, c, :], in0=src, scalar=w, in1=cacc[:, c, :],
                                                       op0=ALU.mult, op1=ALU.add)
                    ins.then_inc(conv_step, 1)
            dve.wait_ge(unit_saved, units_with("mk"))
            for j in range(ML_TAPS):
                for c in range(8):
                    src = m_in[:, c, j:j + T]
                    w = col("mconv_w", 8 * j + c)
                    if j == 0:
                        ins = dve.tensor_scalar(mqk[:, c, :], src, w, col("mconv_b", c), ALU.mult, ALU.add)
                    else:
                        dve.wait_ge(mconv_step, 8 * (j - 1) + c + 1)
                        ins = dve.scalar_tensor_tensor(out=mqk[:, c, :], in0=src, scalar=w, in1=mqk[:, c, :],
                                                       op0=ALU.mult, op1=ALU.add)
                    ins.then_inc(mconv_step, 1)
            dve.wait_ge(unit_saved, units_with("small"))
            dve.wait_ge(bias_loaded, 32)
            fi = gates[:, :, 48:56]
            step(dve.tensor_tensor(fi, fi, fi_b[:, :].unsqueeze(1).broadcast_to([P, TT, 8]), ALU.add))
            ig, fg = gates[:, :, 48:52], gates[:, :, 52:56]
            dve.scalar_tensor_tensor(out=ml[:, 0, :, :], in0=fg, scalar=-1.0, in1=fg, op0=ALU.mult, op1=ALU.min)\
                .then_inc(f_in, 1)
            dve.wait_ge(lf_log, 1)
            dve.scalar_tensor_tensor(out=ml[:, 3, :, :], in0=fg, scalar=0.0, in1=ml[:, 2, :, :], op0=ALU.min,
                                     op1=ALU.subtract).then_inc(lf_ready, 1)
            dve.wait_ge(conv_step, TAPS * CT)
            dve.wait_ge(ln_sum, 1)
            step(dve.tensor_tensor(cacc, cacc, PS[:, 5, 0:T].unsqueeze(1).broadcast_to([P, CT, T]), ALU.subtract))
            dve.tensor_tensor(tmp, cacc, cacc, ALU.mult).then_inc(ln_cen, 1)
            dve.wait_ge(ln_root, 1)
            step(dve.reciprocal(pT[:, 0, 0:T], pT[:, 0, 0:T]))
            dve.tensor_tensor(cacc, cacc, pT[:, 0:1, 0:T].broadcast_to([P, CT, T]), ALU.mult).then_inc(ln_done, 1)
            dve.wait_ge(f_summed, 1)
            B = ml[:, 4, :, :]
            step(dve.tensor_copy(B, PS[:, 4, 0:8].rearrange("p (t h) -> p t h", t=TT)))
            step(dve.tensor_tensor(ml[:, 5, :, :], ig, B, ALU.subtract))
            for t in range(TT):
                ins = dve.tensor_tensor(diag[:, t, :].rearrange("p (h s) -> p h s", h=ML_H),
                                        ident[:, :].unsqueeze(1).broadcast_to([P, ML_H, P]),
                                        ml[:, 5, t, :].unsqueeze(2).broadcast_to([P, ML_H, P]), ALU.mult)
                if t == 0:
                    step(ins)
                else:
                    ins.then_inc(diag_ready, 1)
            dve.wait_ge(mconv_step, 8 * ML_TAPS)
            dve.wait_ge(unit_saved, units_with("vc"))
            for b in range(2):
                for g in range(GROUPS):
                    for half in range(2):
                        r = 64 * (g % 2)
                        base = kcv[r:r + 64, 2 * b + g // 2, :]
                        src = bass.AP(base.tensor, base.offset + half, [list(base.ap[0]), [2, CMP_J], [16, CMP_N]])
                        step(dve.tensor_copy(blk[64 * half:64 * half + 64, b, :, g * CMP_N:(g + 1) * CMP_N], src))
            for b, name in enumerate(("pos_k", "pos_v")):
                pos = par[:, PAR[name]:PAR[name] + CMP_J].unsqueeze(2).broadcast_to([P, CMP_J, 60])
                ins = dve.tensor_tensor(blk[:, b, :, :], blk[:, b, :, :], pos, ALU.add)
                if b == 0:
                    step(ins)
                else:
                    ins.then_inc(blk_ready, 1)
            dve.wait_ge(g_spread, 1)
            spread = [PS[:, b, :].rearrange("p (h s) -> p h s", h=ML_H) for b in (4, 7)]
            mask_h = cmask[:, :].unsqueeze(1).broadcast_to([P, ML_H, P])
            step(dve.tensor_tensor(gmb[:, :, 0, :], spread[0], mask_h, ALU.add))
            step(dve.tensor_copy(gmb[:, :, 1, :], spread[0]))
            step(dve.tensor_tensor(gmb[:, :, 2, :], spread[1], mask_h, ALU.add))
            step(dve.tensor_reduce(ml[:, 6, 0, :], gmb[:, :, 0, :], AX, ALU.max))
            step(dve.tensor_reduce(ml[:, 6, 1, :], gmb[:, :, 1:3, :].rearrange("p h a b -> p h (a b)"), AX, ALU.max))
            step(dve.tensor_scalar(ml[:, 7, :, :], ml[:, 6, :, :], 0.0, -1.0, ALU.max, ALU.mult))
            dve.tensor_tensor(ml[:, 9, :, :], ml[:, 7, :, :], B, ALU.subtract).then_inc(gm_ready, 1)
            for h in range(ML_H):
                dve.wait_ge(qk_done, h + 1)
                dve.wait_ge(decay_ready, 2 * (h + 1))
                flat = gmb[:, h, :, :].rearrange("p a b -> p (a b)")
                dve.scalar_tensor_tensor(out=flat, in0=PS[:, 4 + h, 0:3 * P], scalar=ML_D ** -0.5, in1=flat,
                                         op0=ALU.mult, op1=ALU.mult).then_inc(s_ready, 1)
            dve.wait_ge(s_ready, ML_H)
            step(dve.tensor_reduce(ml[:, 6, 0, :], gmb[:, :, 0, :], AX, ALU.add))
            step(dve.tensor_reduce(ml[:, 6, 1, :], gmb[:, :, 1:3, :].rearrange("p h a b -> p h (a b)"), AX, ALU.add))
            step(dve.tensor_scalar(ml[:, 7, :, :], ml[:, 6, :, :], -1.0, None, ALU.mult))
            step(dve.tensor_tensor(ml[:, 6, :, :], ml[:, 6, :, :], ml[:, 7, :, :], ALU.max))
            dve.wait_ge(decay_ready, 2 * ML_H + 1)
            step(dve.tensor_tensor(ml[:, 6, :, :], ml[:, 6, :, :], ml[:, 8, :, :], ALU.max))
            step(dve.reciprocal(ml[:, 7, :, :], ml[:, 6, :, :]))
            mo_v = mo[:, :, :].rearrange("p t (h d) -> p t h d", h=ML_H)
            dve.wait_ge(unit_saved, units_with("mo"))
            for h in range(ML_H):
                dve.wait_ge(num_done, h + 1)
                for t in range(TT):
                    dve.scalar_tensor_tensor(out=mo_v[:, t, h, :], in0=PS[:, 4 + h, t * P:(t + 1) * P],
                                             scalar=ml[:, 7, t, h:h + 1], in1=mo_v[:, t, h, :], op0=ALU.mult,
                                             op1=ALU.mult).then_inc(hm_ready, 1)
            dve.wait_ge(hm_ready, 2 * ML_H)
            sq = gmb[:, :, :, :].rearrange("p a b c -> p (a b c)")[:, 0:1024].rearrange("p (t h d) -> p t h d", t=TT,
                                                                                         h=ML_H)
            dve.wait_ge(s_turned, ML_H)
            step(dve.tensor_tensor(sq, mo_v, mo_v, ALU.mult))
            dve.tensor_reduce(ml[:, 10, :, :], sq, AX, ALU.add).then_inc(hm_sq, 1)
            dve.wait_ge(hm_root, 1)
            step(dve.reciprocal(ml[:, 11, :, :], ml[:, 11, :, :]))
            dve.tensor_tensor(mo_v, mo_v, ml[:, 11, :, :].unsqueeze(3).broadcast_to([P, TT, ML_H, P]), ALU.mult)\
                .then_inc(hm_norm, 1)

            tile = [0]
            turned = [sum(2 * (ATT[b][2] + 1) + 1 for b in range(a)) for a in range(len(ATT) + 1)]

            def biases(a):
                p, g, t = ATT[a]
                u = a % 2
                if a >= 2:
                    dve.wait_ge(p_turned, turned[a - 1])
                for i in range(HPG):
                    slope = SLOPES[(2 * p + g) * HPG + i]
                    for part in range(t + 1):
                        b = PS[:, tile[0] % 4, :]
                        dve.wait_ge(scored, tile[0] + 1)
                        off = 16 * (part == 0)
                        d = dist[:, 1 if part == t else 0, :].unsqueeze(1).broadcast_to([P, 2, P])
                        if part == 0:
                            dve.scalar_tensor_tensor(out=sc_c[:, u, i, :], in0=dist_c[:, t, :], scalar=slope,
                                                     in1=b[:, 0:16], op0=ALU.mult, op1=ALU.add)
                        dve.scalar_tensor_tensor(out=sc[:, u, i, :, part * P:(part + 1) * P], in0=d, scalar=slope,
                                                 in1=b[:, off:off + 256].rearrange("p (a b) -> p a b", a=2),
                                                 op0=ALU.mult, op1=ALU.add).then_inc(biased, 1)
                        tile[0] += 1
                dve.wait_ge(biased, tile[0])
                w = P * (t + 1)
                step(dve.tensor_reduce(rs[:, u, 0, :, 1:3], sc[:, u, :, :, 0:w], AX, ALU.max, negate=True))
                step(dve.tensor_reduce(rs[:, u, 0, :, 0], sc_c[:, u, :, :], AX, ALU.max, negate=True))
                dve.tensor_scalar(rs[:, u, 0, :, 0], rs[:, u, 0, :, 0], 1.0e20, None, ALU.min).then_inc(max_ready, 1)

            def gated(a):
                p, g, t = ATT[a]
                u, w, G = a % 2, P * (t + 1), 2 * p + g
                dve.wait_ge(exp_done, a + 1)
                r = rs[:, u, 2, :, :]
                step(dve.tensor_scalar(r, rs[:, u, 1, :, :], 1.0e-30, None, ALU.max))
                step(dve.reciprocal(r, r))
                step(dve.tensor_tensor(r, r, gates[:, t, G * 12:(G + 1) * 12].rearrange("p (i b) -> p i b", i=HPG),
                                       ALU.mult))
                for i in range(HPG):
                    for br in range(2):
                        s = sc[:, u, i, br, 0:w]
                        ins = dve.tensor_scalar(s, s, rs[:, u, 2, i, 1 + br:2 + br], None, ALU.mult)
                s = sc_c[:, u, :, :]
                dve.tensor_tensor(s, s, rs[:, u, 2, :, 0:1].broadcast_to([P, HPG, 16]), ALU.mult).then_inc(p_ready, 1)

            biases(0)
            for a in range(len(ATT)):
                if a + 1 < len(ATT):
                    biases(a + 1)
                gated(a)
            dve.wait_ge(o_saved, len(ATT))
            dve.wait_ge(p_turned, turned[-1])
            heads = mix[:, 0:8, :].rearrange("p a b -> p (a b)")
            for c in range(4):
                o = heads[:, c * 512:(c + 1) * 512]
                dve.tensor_tensor(osq[:, c * 512:(c + 1) * 512], o, o, ALU.mult).then_inc(osq_ready, 1)
            for c in range(4):
                r = oroot_b[:, c * 512:(c + 1) * 512]
                o = heads[:, c * 512:(c + 1) * 512]
                dve.wait_ge(oroot, c + 1)
                step(dve.reciprocal(r, r))
                step(dve.tensor_tensor(o, o, r, ALU.mult))
                for k in (2 * c, 2 * c + 1):
                    dve.tensor_scalar(mix[:, k, :], mix[:, k, :], col("nsa_g", k), None, ALU.mult)\
                        .then_inc(attn_out, 1)
            for v in range(4 * TT):
                m, t = v // TT, v % TT
                dve.wait_ge(out_done, v + 1)
                y = x1[:, t, m * 512:(m + 1) * 512]
                dve.tensor_tensor(y, PS[:, 4 + v % 4, :], y, ALU.add).then_inc(out_added, 1)

            dve.wait_ge(gain_loaded, 16)
            dve.wait_ge(ffn_root, 1)
            step(dve.reciprocal(st[:, 8:10], st[:, 8:10]))
            for t in range(TT):
                for c in range(4):
                    ins = dve.scalar_tensor_tensor(
                        out=xn[:, t, 4 * c:4 * c + 4, :].rearrange("t j p -> t p j"),
                        in0=x1[:, t, c * 512:(c + 1) * 512].rearrange("t (p j) -> t p j", j=4),
                        scalar=st[:, 8 + t:9 + t],
                        in1=fin_g[:, c * 512:(c + 1) * 512].rearrange("t (p j) -> t p j", j=4),
                        op0=ALU.mult, op1=ALU.mult)
                ins.then_inc(xn_ready, 1)
            dve.memset(SW[:, 1, :], 0.0)
            dve.memset(Y2[:, 1, :], 0.0).then_inc(zeroed, 1)
            step(dve.memset(rank[:, :, E:], -1.0))
            step(dve.memset(wgt[:, :, E:], 0.0))

            dve.wait_ge(logits_done, 1)
            dve.wait_ge(router_loaded, 16 * ROUTER_DMAS)
            Lg, Le = ro[:, 8, :, 0:EG], ro[:, 1, :, :]
            lg = PS[:, 4, 0:128].rearrange("p (t n) -> p t n", t=TT)
            step(dve.tensor_tensor(Lg, lg[:, :, 0:EG], rout_b[:, 0:EG].unsqueeze(1).broadcast_to([P, TT, EG]), ALU.add))
            step(dve.tensor_tensor(Le, lg[:, :, EG:EG + E],
                                   rout_b[:, EG:EG + E].unsqueeze(1).broadcast_to([P, TT, E]), ALU.add))

            def wide(v, n):
                return rt[:, v, :].unsqueeze(2).broadcast_to([P, TT, n])

            def pick(one, scores_, top, n, low):
                step(dve.tensor_reduce(rt[:, top, :], scores_, AX, ALU.max))
                step(dve.tensor_tensor(one, scores_, wide(top, n), ALU.is_equal))
                step(dve.tensor_tensor(one, one, low.unsqueeze(1).broadcast_to([P, TT, n]), ALU.mult))
                step(dve.tensor_reduce(rt[:, 15, :], one, AX, ALU.max))
                step(dve.tensor_tensor(one, one, wide(15, n), ALU.is_equal))

            og = ro[:, 9, :, 0:EG]
            pick(og, Lg, 0, EG, countdown[:, 0:EG])
            step(dve.tensor_tensor(ro[:, 6, :, 0:EG], Lg, wide(0, EG), ALU.subtract))
            step(dve.tensor_scalar(og, og, -NEG, NEG, ALU.mult, ALU.add))
            for t in range(TT):
                e4 = Le[:, t, :].rearrange("p (g e) -> p g e", g=EG)
                step(dve.tensor_tensor(e4, e4, og[:, t, :].unsqueeze(2).broadcast_to([P, EG, EI]), ALU.add))
            one1, one2, rest = ro[:, 2, :, :], ro[:, 3, :, :], ro[:, 4, :, :]
            pick(one1, Le, 1, E, countdown[:, :])
            step(dve.scalar_tensor_tensor(out=rest, in0=one1, scalar=3 * NEG, in1=Le, op0=ALU.mult, op1=ALU.add))
            pick(one2, rest, 2, E, countdown[:, :])
            dve.tensor_tensor(rt[:, 9, :], rt[:, 2, :], rt[:, 1, :], ALU.subtract).then_inc(route_max, 1)
            dve.wait_ge(route_exp, 2)
            step(dve.tensor_reduce(rt[:, 3, :], ro[:, 7, :, 0:EG], AX, ALU.add))
            step(dve.reciprocal(rt[:, 4, :], rt[:, 3, :]))
            step(dve.tensor_scalar(rt[:, 5, :], rt[:, 10, :], 1.0, None, ALU.add))
            step(dve.reciprocal(rt[:, 6, :], rt[:, 5, :]))
            step(dve.tensor_tensor(rt[:, 7, :], rt[:, 4, :], rt[:, 6, :], ALU.mult))
            step(dve.tensor_tensor(rt[:, 8, :], rt[:, 7, :], rt[:, 10, :], ALU.mult))
            A = ro[:, 0, :, :]
            dve.tensor_tensor(A, one1, one2, ALU.add).then_inc(picks_ready, 1)
            step(dve.tensor_tensor(ro[:, 5, :, :], one1, wide(7, E), ALU.mult))
            step(dve.tensor_tensor(ro[:, 10, :, :], one2, wide(8, E), ALU.mult))
            step(dve.tensor_tensor(wgt[:, :, 0:E], ro[:, 5, :, :], ro[:, 10, :, :], ALU.add))
            dve.wait_ge(ranks_done, 1)
            rk = PS[:, 5, 0:128].rearrange("p (t n) -> p t n", t=TT)[:, :, 0:E]
            step(dve.scalar_tensor_tensor(out=rank[:, :, 0:E], in0=rk, scalar=1.0, in1=A, op0=ALU.add, op1=ALU.mult))
            dve.tensor_scalar(rank[:, :, 0:E], rank[:, :, 0:E], -1.0, None, ALU.add).then_inc(counts_ready, 1)
            dve.tensor_copy(cnt[:, :], PS[0:1, 6, 0:E]).then_inc(counts_ready, 1)
            dve.wait_ge(counts_ready, 2)

            HT = PS[:, 1, :].rearrange("p (k n) -> p k n", k=4)

            def add_scattered(t, cols, done):
                y = x1[:, t, cols * 1024:(cols + 1) * 1024]
                dve.tensor_tensor(y, PS[:, 4:6, :].rearrange("p a b -> p (a b)"), y, ALU.add).then_inc(done, 1)

            def select(first, count):
                for t in range(TT):
                    dve.tensor_tensor(sel[:, t, :, :], slot_id[:, :].unsqueeze(1).broadcast_to([P, QUAD, SLOTS]),
                                      rank[:, t, bass.ds(first, QUAD)].unsqueeze(2).broadcast_to([P, QUAD, SLOTS]),
                                      ALU.is_equal).then_inc(sel_made, 1)
                dve.wait_ge(sel_made, count * TT + TT)
                for t in range(TT):
                    ins = dve.tensor_tensor(
                        selw[:, t, :, :], sel[:, t, :, :],
                        wgt[:, t, bass.ds(first, QUAD)].unsqueeze(2).broadcast_to([P, QUAD, SLOTS]), ALU.mult)
                ins.then_inc(sel_ready, 1)

            select(0, 0)
            for counted in (y_saved_d, sc_added, hid_ready):
                dve.sem_inc(counted, 1)
            with dve.Fori(0, NQUAD) as q:
                for i in range(QUAD):
                    dve.wait_ge(sc_filled, q * 8 + (2 * i + 1))
                    add_scattered(i % 2, 0, sc_added)
                    dve.wait_ge(silu_done, q * QUAD + (i + 1))
                    dve.tensor_tensor(hTe[:, :, :], HT[:, :, SLOTS:2 * SLOTS], sg[:, :, :], ALU.mult)\
                        .then_inc(hid_ready, 1)
                    dve.wait_ge(sc_filled, q * 8 + (2 * i + 2))
                    add_scattered(i % 2, 1, sc_added)
                    dve.wait_ge(w_used[5], q * QUAD + (i + 1))
                    r = 64 * (i % 2)
                    dve.tensor_copy(Y2[r:r + 64, i // 2, 1024:2048],
                                    PS[64:128, 2:4, :].rearrange("p a b -> p (a b)")).then_inc(y_saved_d, 1)
                    if i == 2:
                        dve.wait_ge(sw_filled, q + 1)
                        select(q * QUAD + QUAD, q + 1)
            for t in range(TT):
                for cols in range(2):
                    dve.wait_ge(sc_filled, 8 * NQUAD + 2 * t + cols + 1)
                    add_scattered(t, cols, sc_added)
            dve.wait_ge(sc_added, 8 * NQUAD + 5)

            OVS = 3 * (ROUNDS - 1) + 1
            with dve.Fori(0, E) as e:
                n = dve.value_load(cnt[0:1, bass.ds(e, 1)], min_val=0, max_val=T)
                with dve.If(n > SLOTS):
                    with dve.Fori(0, ROUNDS - 1) as r:
                        at0 = e * (ROUNDS - 1) + r
                        dve.tensor_scalar(slot_id[:, :], slot_id[:, :], float(SLOTS), None, ALU.add)\
                            .then_inc(ov_step, 1)
                        dve.wait_ge(ov_step, e * OVS + r * 3 + 1)
                        for t in range(TT):
                            dve.tensor_tensor(sel[:, t, 0, :], slot_id[:, :],
                                              rank[:, t, bass.ds(e, 1)].broadcast_to([P, SLOTS]),
                                              ALU.is_equal).then_inc(ov_step, 1)
                        dve.wait_ge(ov_step, e * OVS + r * 3 + 3)
                        for t in range(TT):
                            ins = dve.tensor_tensor(selw[:, t, 0, :], sel[:, t, 0, :],
                                                    wgt[:, t, bass.ds(e, 1)].broadcast_to([P, SLOTS]), ALU.mult)
                        ins.then_inc(ov_sel, 1)
                        dve.wait_ge(ov_pe, at0 * OV_PE + 10)
                        dve.wait_ge(ov_act, at0 * OV_ACT + 10)
                        dve.tensor_tensor(hTe[:, :, :], HT[:, :, SLOTS:2 * SLOTS], sg[:, :, :], ALU.mult)\
                            .then_inc(ov_dve, 1)
                        for s in range(4):
                            dve.wait_ge(ov_pe, at0 * OV_PE + (13 + s))
                            add_scattered(s // 2, s % 2, ov_dve)
                    dve.wait_ge(ov_dve, (e * (ROUNDS - 1) + (ROUNDS - 1)) * OV_DVE)
                    dve.tensor_scalar(slot_id[:, :], slot_id[:, :], -float(SLOTS * (ROUNDS - 1)), None, ALU.add)\
                        .then_inc(ov_step, 1)
                    dve.wait_ge(ov_step, e * OVS + OVS)
                    dve.sem_inc(ov_end, 1)
                with dve.Else():
                    dve.sem_inc(ov_dve, (ROUNDS - 1) * OV_DVE)
                    dve.sem_inc(ov_sel, ROUNDS - 1)
                    dve.sem_inc(ov_step, OVS)
                    dve.sem_inc(ov_end, 1)

            dve.wait_ge(fing_loaded, 16)
            dve.wait_ge(fin_root, 1)
            step(dve.reciprocal(st[:, 12:14], st[:, 12:14]))
            for t in range(TT):
                dve.scalar_tensor_tensor(out=x1[:, t, :], in0=x1[:, t, :], scalar=st[:, 12 + t:13 + t],
                                         in1=fin_g[:, :], op0=ALU.mult, op1=ALU.mult).then_inc(fin_ready, 1)


_INS = ['x', 'attn_norm_g', 'w_in', 'cmp_pos_k', 'cmp_w1_k', 'cmp_w2_k', 'cmp_pos_v', 'cmp_w1_v', 'cmp_w2_v',
        'nsa_out_g', 'mlstm_conv_w', 'mlstm_conv_b', 'mlstm_i_bias', 'mlstm_f_bias', 'mlstm_out_g', 'conv_w',
        'conv_b', 'conv_ln_g', 'conv_ln_b', 'w_out', 'ffn_norm_g', 'router_w_group', 'router_b_group',
        'router_w_expert', 'router_b_expert', 'expert_w_gate', 'expert_w_up', 'expert_w_down', 'final_norm_g']
_OUTS = [((1, T, D), 'float32')]


def kernel(**inputs):
    import numpy as _np
    import concourse.bacc as _bacc
    from concourse import mybir as _mybir
    from concourse.bass_utils import run_bass_kernel_spmd as _run

    nc = _bacc.Bacc("TRN2", target_bir_lowering=False, num_devices=1)
    arrays, args = {}, []
    for name in _INS:
        a = _np.ascontiguousarray(inputs[name])
        arrays[f"in_{name}_dram"] = a
        args.append(nc.dram_tensor(f"in_{name}_dram", a.shape, _mybir.dt.from_np(a.dtype), kind="ExternalInput").ap())
    for i, (shape, dtype) in enumerate(_OUTS):
        dt = _mybir.dt.from_np(_np.dtype(dtype))
        args.append(nc.dram_tensor(f"out_{i}_dram", shape, dt, kind="ExternalOutput").ap())
    build(nc, *args)
    r = _run(nc, [arrays], core_ids=[0])
    got = tuple(r.results[0][f"out_{i}_dram"] for i in range(len(_OUTS)))
    return got[0]
```

```python
from contextlib import ExitStack

import concourse.bass as bass
import numpy as np
from concourse import mybir

F32 = mybir.dt.float32
I32 = mybir.dt.int32
ALU = mybir.AluOpType
ACT = mybir.ActivationFunctionType
AX = mybir.AxisListType.X

P = 128
T = 256
TT = T // P
D = 2048
DK = D // P
DH = 64
HEADS, GROUPS, HPG = 16, 4, 4
CMP_N, CMP_J = 15, 16
ML_H, ML_D = 4, 128
CT = 4
TAPS, ML_TAPS = 31, 4
EPS, LN_EPS = 1e-6, 1e-5
NEG = -1.0e30
E, EG, EI = 32, 4, 8
SLOTS = 64
RING = 6
QUAD = 4
NQUAD = E // QUAD
CHUNKS = 6
BLOCKS = (2 * T - 1) // SLOTS
PAR_DMAS = 14
ROUTER_DMAS = 11
OV_PE, OV_ACT, OV_DVE = 16, 13, 5
OV_BANK = [4, 2, 4, 2]

WIDTH = dict(q=1024, kc=256, vc=256, ks=256, vs=256, kw=256, vw=256, gate=48, mq=512, mk=512, mv=512, mo=512,
             mi=4, mf=4, ca=512, cg=512)
COL = dict(zip(WIDTH, np.cumsum([0] + list(WIDTH.values()))[:-1].tolist()))
SMALL = WIDTH["gate"] + WIDTH["mi"] + WIDTH["mf"]

SLABS = ["cg0", "cg1", "ca0", "ca1", "mq0", "mq1", "mk0", "mk1", "small", "kc0", "vc0", "ks0", "kw0",
         "w1k", "w1v", "vs0", "q0", "q1", "q2", "q3", "vw0", "mv0", "mv1", "mo0", "mo1"]


def projection_units():
    units = []
    for n, name in enumerate(SLABS):
        part, s = (name, 0) if name in ("small", "w1k", "w1v") else (name[:-1], int(name[-1]))
        if part in ("small", "mv", "mo", "vs", "vw"):
            units += [(n, part, "rows", s, t) for t in range(TT)]
        elif part in ("w1k", "w1v"):
            units.append((n, part, "hidden", 0, 0))
        elif part == "q":
            if s % 2:
                units += [(n, part, "heads", s // 2, i) for i in range(HPG)]
        else:
            units += [(n, part, "columns", s, i) for i in range(2)]
    return units


UNITS = projection_units()


def units_through(slab):
    if SLABS[slab] in ("q0", "q2"):
        slab += 1
    return max(u for u, unit in enumerate(UNITS) if unit[0] == slab) + 1


def units_before(part):
    return min(u for u, unit in enumerate(UNITS) if unit[1] == part)


def units_with(part):
    return max(u for u, unit in enumerate(UNITS) if unit[1] == part) + 1


LATE = units_before("mv")


def unit_bank(u):
    return u % 4 if u < LATE else u % 2


OUT_SLOTS = [(1, 2), (3, 4), (0, 5), (1, 2)]
OUT_DMAS = 10
CHUNK_SLOT = [3, 4, 0, 5, 1, 2]
CHUNK_DMAS = [2, 2, 2, 2, 1, 1]
CHUNK_INC = [16 * n for n in CHUNK_DMAS]

PAR = {}
_at = 0
for _name, _n in (("attn_g", 16), ("nsa_g", 8), ("ml_g", 4), ("mconv_w", 32), ("mconv_b", 8), ("conv_b", 4),
                  ("ln_g", 4), ("ln_b", 4), ("pos_k", 16), ("pos_v", 16)):
    PAR[_name] = _at
    _at += _n
PAR_ROWS = _at
TAP_ROWS = TAPS * CT

def after(part, n):
    return units_before(part) + n


BETWEEN_PE = {after("kc", 1): ["forget_sum", "ln_mean"], after("vc", 1): ["ln_square"],
              after("ks", 1): ["spread_gates"], after("vs", 0): ["mlstm_scores"],
              after("q", 1): ["hidden_columns"], after("q", 5): ["compressed"]}
BETWEEN_ACT = {after("kc", 0): ["conv_silu"], after("kc", 1): ["forget_logs"], after("vc", 1): ["ln_std"],
               after("kw", 0): ["conv_result"], after("vs", 0): ["decays"], after("q", 1): ["hidden_save"],
               after("q", 5): ["compressed_save"]}

KEYS = 16 + 2 * 256
ATT = [(p, g, t) for p in range(2) for t in range(TT) for g in range(2)]
SLOPES = [2.0 ** (-8.0 * (h + 1) / HEADS) for h in range(HEADS)]


def build(nc, x, attn_norm_g, w_in, cmp_pos_k, cmp_w1_k, cmp_w2_k, cmp_pos_v, cmp_w1_v, cmp_w2_v, nsa_out_g,
          mlstm_conv_w, mlstm_conv_b, mlstm_i_bias, mlstm_f_bias, mlstm_out_g, conv_w, conv_b, conv_ln_g,
          conv_ln_b, w_out, ffn_norm_g, router_w_group, router_b_group, router_w_expert, router_b_expert,
          expert_w_gate, expert_w_up, expert_w_down, final_norm_g, out):
    with ExitStack() as ctx:
        def sb(name, shape, dt=F32, stack=ctx):
            return stack.enter_context(nc.sbuf_tensor(name, shape, dt))

        def sem(name):
            return ctx.enter_context(nc.semaphore(name))

        PS = ctx.enter_context(nc.psum_tensor("PS", [P, 8, 512], F32))

        ring = sb("ring", [P, RING, DK, 256])
        x1 = sb("x1", [P, TT, D])
        ident = sb("ident", [P, P])
        ones = sb("ones", [P, P])
        upto = sb("upto", [P, P])
        before = sb("before", [P, P])
        small_c = sb("small_c", [P, 8])
        EPS_C, LN_EPS_C, ONE_C, ZERO_C = (small_c[:, i:i + 1] for i in range(4))
        st = sb("st", [P, 16])
        countdown = sb("countdown", [P, E])
        slot_id = sb("slot_id", [P, SLOTS])
        row_id = sb("row_id", [E, 1])
        ffn_gc = sb("ffn_gc", [P, 4, 4])
        ssq = sb("ssq", [P, TT, 4])
        rout_b = sb("rout_b", [P, EG + E])
        roww = sb("roww", [P, DK, EG + E])

        mixer = ExitStack()

        def mb(name, shape, dt=F32):
            return sb(name, shape, dt, mixer)

        mix = mb("mix", [P, DK, T])
        hn = mix[:, :, :].rearrange("p a b -> p (a b)").rearrange("p (t d) -> p t d", t=TT)
        mqk = mix[:, 0:8, :]
        cgs = mix[:, 8:12, :]
        cacc = mix[:, 12:16, :]
        hT = mb("hT", [P, DK, T])
        nsa_q = mb("nsa_q", [P, 8, T])
        tmp = nsa_q[:, 0:4, :]
        diag = nsa_q[:, 4:8, :].rearrange("p a b -> p (a b)").rearrange("p (t n) -> p t n", t=TT)
        keys = mb("keys", [P, 2, KEYS])
        vals = mb("vals", [P, 2, TT, 256])
        gates = mb("gates", [P, TT, SMALL])
        fi_b = mb("fi_b", [P, 8])
        par = mb("par", [P, PAR_ROWS])
        taps = mb("taps", [P, TAP_ROWS])
        vcs = mb("vcs", [32, GROUPS, DH])
        w2 = mb("w2", [P, 2, 2, DH])
        cmask = mb("cmask", [P, P])
        dist = mb("dist", [P, 2, P])
        dist_c = mb("dist_c", [P, TT, 16])
        av_ln = vals[:, 1, 1, 0:P]
        av_hd = mb("av_hd", [P, P])
        ml = mb("ml", [P, 12, TT, ML_H])
        gmb = mb("gmb", [P, ML_H, 3, P])
        prow, trow = gmb[:, 0, 0, :], gmb[:, 0, 1, :]
        kcv = gmb[:, :, :, :].rearrange("p a b c -> p (a b c)")[:, 0:1024].rearrange("p (a b) -> p a b", a=4)
        mv = mb("mv", [P, TT, 512])
        mo = mb("mo", [P, TT, 512])
        pT = mb("pT", [P, 2, 512])
        hid = mb("hid", [P, 512])
        att = mb("att", [P, 4096])
        cin = att[:, 0:CT * 286].rearrange("p (c t) -> p c t", c=CT)
        m_in = att[:, 1152:1152 + 8 * 259].rearrange("p (c t) -> p c t", c=8)
        blk = att[:, 1152:1152 + 2 * CMP_J * 60].rearrange("p (b j n) -> p b j n", b=2, j=CMP_J)
        sc = att[:, :].rearrange("p (u h b k) -> p u h b k", u=2, h=HPG, b=2)
        osq = att[:, 0:2048]
        oroot_b = att[:, 2048:4096]
        sc_c = mb("sc_c", [P, 2, HPG, 16])
        rs = mb("rs", [P, 2, 3, HPG, 3])
        mixer.close()

        xn = sb("xn", [P, TT, DK, P])
        XG = sb("XG", [P, DK, QUAD * SLOTS])
        Y2 = sb("Y2", [P, 2, D])
        sel = sb("sel", [P, TT, QUAD, SLOTS])
        selw = sb("selw", [P, TT, QUAD, SLOTS])
        SW = sb("SW", [P, 2, T])
        Hs = sb("Hs", [P, 512])
        sg = sb("sg", [P, 4, SLOTS])
        hTe = sb("hTe", [P, 4, SLOTS])
        fin_g = sb("fin_g", [P, D])
        ro = sb("ro", [P, 12, TT, E])
        rt = sb("rt", [P, 16, TT])
        rank = sb("rank", [P, TT, E + QUAD])
        wgt = sb("wgt", [P, TT, E + QUAD])
        ovt = sb("ovt", [E, 4])
        own = sb("own", [E, 3, BLOCKS])
        blk_f = sb("blk_f", [P, 3 * BLOCKS])
        blk_i = sb("blk_i", [1, 3 * BLOCKS], I32)
        xnT = XG
        ffn_g = Y2[:, 0, :]

        x_loaded = sem("x_loaded")
        par_loaded = sem("par_loaded")
        small_loaded = sem("small_loaded")
        w2_loaded = sem("w2_loaded")
        bias_loaded = sem("bias_loaded")
        router_loaded = sem("router_loaded")
        gain_loaded = sem("gain_loaded")
        fing_loaded = sem("fing_loaded")
        w_loaded = [sem(f"w_loaded{s}") for s in range(RING)]
        const_step = sem("const_step")
        consts_ready = sem("consts_ready")
        ssq_ready = sem("ssq_ready")
        rstd_root = sem("rstd_root")
        hn_ready = sem("hn_ready")
        par_turned = sem("par_turned")
        par_ready = sem("par_ready")
        h_turned = sem("h_turned")
        hT_ready = sem("hT_ready")
        unit_done = sem("unit_done")
        unit_saved = sem("unit_saved")
        pads_ready = sem("pads_ready")
        conv_gated = sem("conv_gated")
        conv_step = sem("conv_step")
        ln_sum = sem("ln_sum")
        ln_sq = sem("ln_sq")
        ln_cen = sem("ln_cen")
        ln_root = sem("ln_root")
        ln_done = sem("ln_done")
        conv_out = sem("conv_out")
        mconv_step = sem("mconv_step")
        mconv_out = sem("mconv_out")
        dve_step = sem("dve_step")
        act_step = sem("act_step")
        lf_ready = sem("lf_ready")
        lf_exp = sem("lf_exp")
        lf_log = sem("lf_log")
        f_in = sem("f_in")
        f_summed = sem("f_summed")
        diag_ready = sem("diag_ready")
        g_spread = sem("g_spread")
        gm_ready = sem("gm_ready")
        decay_ready = sem("decay_ready")
        qk_done = sem("qk_done")
        s_ready = sem("s_ready")
        s_turned = sem("s_turned")
        sT_ready = sem("sT_ready")
        num_done = sem("num_done")
        hm_ready = sem("hm_ready")
        hm_sq = sem("hm_sq")
        hm_root = sem("hm_root")
        hm_norm = sem("hm_norm")
        hm_turned = sem("hm_turned")
        hm_out = sem("hm_out")
        blk_ready = sem("blk_ready")
        hid_turned = sem("hid_turned")
        hidT_ready = sem("hidT_ready")
        cmp_done = sem("cmp_done")
        cmp_saved = sem("cmp_saved")
        scored = sem("scored")
        biased = sem("biased")
        max_ready = sem("max_ready")
        exp_done = sem("exp_done")
        p_ready = sem("p_ready")
        p_turned = sem("p_turned")
        pT_ready = sem("pT_ready")
        pv_done = sem("pv_done")
        o_saved = sem("o_saved")
        osq_ready = sem("osq_ready")
        oms_done = sem("oms_done")
        oroot = sem("oroot")
        o_normed = sem("o_normed")
        attn_out = sem("attn_out")
        out_done = sem("out_done")
        out_added = sem("out_added")
        ffn_ssq = sem("ffn_ssq")
        ffn_root = sem("ffn_root")
        xn_ready = sem("xn_ready")
        xn_turned = sem("xn_turned")
        xnT_ready = sem("xnT_ready")
        logits_done = sem("logits_done")
        route_max = sem("route_max")
        route_exp = sem("route_exp")
        picks_ready = sem("picks_ready")
        ranks_done = sem("ranks_done")
        blocks_step = sem("blocks_step")
        blocks_pe = sem("blocks_pe")
        blocks_ready = sem("blocks_ready")
        roww_ready = sem("roww_ready")
        ffn_summed = sem("ffn_summed")
        zeroed = sem("zeroed")
        sel_made = sem("sel_made")
        sel_ready = sem("sel_ready")
        g_filled = sem("g_filled")
        g_saved = sem("g_saved")
        w_used = [sem(f"w_used{c}") for c in range(CHUNKS)]
        h_saved = sem("h_saved")
        h_turned_e = sem("h_turned_e")
        silu_done = sem("silu_done")
        hid_ready = sem("hid_ready")
        y_saved_a = sem("y_saved_a")
        y_saved_d = sem("y_saved_d")
        sw_filled = sem("sw_filled")
        sw_saved = sem("sw_saved")
        sc_filled = sem("sc_filled")
        sc_added = sem("sc_added")
        ov_loaded = [sem(f"ov_loaded{c}") for c in range(CHUNKS)]
        ov_step = sem("ov_step")
        ov_sel = sem("ov_sel")
        ov_pe = sem("ov_pe")
        ov_act = sem("ov_act")
        ov_dve = sem("ov_dve")
        ov_end = sem("ov_end")
        ov_left = sem("ov_left")
        fin_ssq = sem("fin_ssq")
        fin_root = sem("fin_root")
        fin_ready = sem("fin_ready")
        stored = sem("stored")

        block = ctx.enter_context(nc.Block())

        w_in_v = w_in[0].rearrange("(k p) n -> p k n", p=P)
        w1_v = {"w1k": cmp_w1_k[0].rearrange("(k p) n -> p k n", p=P),
                "w1v": cmp_w1_v[0].rearrange("(k p) n -> p k n", p=P)}
        wo_heads = w_out[0, 0:1024, :].rearrange("(p g i d) n -> p g d i n", p=2, g=2, i=HPG)
        wo_rest = w_out[0, 1024:2048, :].rearrange("(k p) n -> p k n", p=P)
        ring_flat = ring[:, :, :, :].rearrange("p s k n -> p s (k n)")
        gate_v = expert_w_gate[0].rearrange("e (c p j) n -> e c p (j n)", c=4, j=4)
        up_v = expert_w_up[0].rearrange("e (c p j) n -> e c p (j n)", c=4, j=4)
        down_v = expert_w_down[0].rearrange("e (c j p) n -> e c p j n", c=2, j=2)

        def chunk_parts(e, c):
            dst = ring_flat[:, CHUNK_SLOT[c], :]
            pick = slice(e, e + 1) if isinstance(e, int) else e
            if c < 4:
                return [(dst[:, 0:2048], gate_v[pick, c].rearrange("e p n -> (e p) n")),
                        (dst[:, 2048:4096], up_v[pick, c].rearrange("e p n -> (e p) n"))]
            return [(dst.rearrange("p (j n) -> p j n", j=2), down_v[pick, c - 4].rearrange("e p j n -> (e p) j n"))]

        def rows_of(dram, n):
            return dram.rearrange("(r c) -> r c", r=n)

        slot_total = [0] * RING
        slab_at = []
        for n in range(len(SLABS)):
            slot_total[n % RING] += 16
            slab_at.append(slot_total[n % RING])
        out_at = []
        for first, _ in OUT_SLOTS:
            slot_total[first] += 16 * OUT_DMAS
            out_at.append(slot_total[first])

        @block.sync
        def _(sp):
            for t in range(TT):
                sp.dma_start(x1[:, t, :], x[0, t * P:(t + 1) * P, :]).then_inc(x_loaded, 16)
            sp.wait_ge(par_loaded, 16 * PAR_DMAS)
            for n, name in enumerate(SLABS):
                if n >= RING:
                    sp.wait_ge(unit_done, units_through(n - RING))
                dst = ring[:, n % RING, :, :]
                if name == "small":
                    gate = COL["gate"]
                    ig = COL["mi"]
                    sp.dma_start(dst[:, :, 0:48], w_in_v[:, :, gate:gate + 48]).then_inc(small_loaded, 16)
                    sp.dma_start(dst[:, :, 48:56], w_in_v[:, :, ig:ig + 8]).then_inc(w_loaded[n % RING], 16)
                elif name in w1_v:
                    sp.dma_start(dst, w1_v[name]).then_inc(w_loaded[n % RING], 16)
                else:
                    c = COL[name[:-1]] + 256 * int(name[-1])
                    sp.dma_start(dst, w_in_v[:, :, c:c + 256]).then_inc(w_loaded[n % RING], 16)
            last_use = {n % RING: units_through(n) for n in range(len(SLABS))}
            for m, pair in enumerate(OUT_SLOTS):
                if m < 3:
                    sp.wait_ge(unit_done, max(last_use[s] for s in pair))
                else:
                    sp.wait_ge(out_done, TT)
                for half, s in enumerate(pair):
                    cols = slice(512 * m + 256 * half, 512 * m + 256 * half + 256)
                    for p in range(2):
                        for g in range(2):
                            sp.dma_start(ring[64 * g:64 * g + 64, s, 4 * p:4 * p + 4, :],
                                         wo_heads[p, g, :, :, cols]).then_inc(w_loaded[pair[0]], 16)
                    sp.dma_start(ring[:, s, 8:16, :], wo_rest[:, :, cols]).then_inc(w_loaded[pair[0]], 16)

            def load_chunk(e, c, done, by=16):
                for dst, src in chunk_parts(e, c):
                    sp.dma_start(dst, src).then_inc(done, by)

            for c in range(CHUNKS):
                sp.wait_ge(out_done, TT * [2, 2, 3, 3, 4, 4][c])
                load_chunk(0, c, w_loaded[CHUNK_SLOT[c]])
            looped = (E - 1) // QUAD
            with sp.Fori(0, looped) as q:
                for i in range(1, QUAD + 1):
                    for c in range(CHUNKS):
                        sp.wait_ge(w_used[c], q * QUAD + i)
                        load_chunk(bass.ds(q * QUAD + i, 1), c, w_loaded[CHUNK_SLOT[c]])
            for e in range(looped * QUAD + 1, E):
                for c in range(CHUNKS):
                    sp.wait_ge(w_used[c], e)
                    load_chunk(e, c, w_loaded[CHUNK_SLOT[c]])

            sp.wait_ge(blocks_ready, 2)
            with sp.Fori(0, BLOCKS) as b:
                active = sp.value_load(blk_i[0:1, bass.ds(b + 2 * BLOCKS, 1)], min_val=0, max_val=1)
                e = sp.value_load(blk_i[0:1, bass.ds(b, 1)], min_val=0, max_val=E - 1)
                with sp.If(active > 0):
                    for c in range(CHUNKS):
                        sp.wait_ge(w_used[c], E)
                        load_chunk(bass.ds(e, 1), c, ov_loaded[c])
                    sp.wait_ge(ov_end, b + 1)
                    sp.sem_inc(ov_left, 1)
                with sp.Else():
                    for c in range(CHUNKS):
                        sp.sem_inc(ov_loaded[c], CHUNK_INC[c])
            for t in range(TT):
                sp.wait_ge(fin_ready, t + 1)
                sp.dma_start(out[0, t * P:(t + 1) * P, :], x1[:, t, :]).then_inc(stored, 16)
            sp.wait_ge(stored, 16 * TT)

        @block.gpsimd
        def _(pool):
            done = [0]

            def step(ins):
                done[0] += 1
                ins.then_inc(const_step, 1)
                pool.wait_ge(const_step, done[0])

            def triangle(tile, base, fill, col, row, op=ALU.is_ge):
                step(pool.affine_select(out=tile, in_=tile, compare_op=op, fill=fill, base=base,
                                        pattern=[[col, tile.shape[1]]], channel_multiplier=row))

            step(pool.memset(ident[:, :], 0.0))
            triangle(ident[:, :], 0, 1.0, -1, 1, ALU.not_equal)
            step(pool.memset(ones[:, :], 1.0))
            for i, v in enumerate((EPS, LN_EPS, 1.0, 0.0)):
                step(pool.memset(small_c[:, i:i + 1], v))
            pool.memset(hid[:, :], 0.0).then_inc(consts_ready, 1)
            step(pool.memset(upto[:, :], 1.0))
            triangle(upto[:, :], 0, 0.0, 1, -1)
            step(pool.memset(before[:, :], 1.0))
            triangle(before[:, :], -1, 0.0, 1, -1)
            step(pool.memset(cmask[:, :], 0.0))
            triangle(cmask[:, :], 0, NEG, -1, 1)
            for i in range(2):
                step(pool.iota(dist[:, i, :], [[1, P]], base=-P * (1 - i), channel_multiplier=-1,
                               allow_small_or_imprecise_dtypes=True))
            triangle(dist[:, 1, :], 0, NEG, -1, 1)
            for t in range(TT):
                step(pool.iota(dist_c[:, t, :], [[16, 16]], base=31 - P * t, channel_multiplier=-1,
                               allow_small_or_imprecise_dtypes=True))
                triangle(dist_c[:, t, :], P * t - 31, NEG, -16, 1)
            step(pool.memset(dist_c[:, :, CMP_N:16], NEG))
            step(pool.memset(av_ln, 1.0 / (CT * P)))
            step(pool.memset(av_hd[:, :], 0.0))
            for h in (0, 64):
                step(pool.memset(av_hd[h:h + 64, h:h + 64], 1.0 / DH))
            step(pool.iota(countdown[:, :], [[-1, E]], base=E, channel_multiplier=0,
                           allow_small_or_imprecise_dtypes=True))
            step(pool.iota(slot_id[:, :], [[1, SLOTS]], base=0, channel_multiplier=0,
                           allow_small_or_imprecise_dtypes=True))
            step(pool.iota(row_id[:, :], [[0, 1]], base=0, channel_multiplier=1,
                           allow_small_or_imprecise_dtypes=True))
            step(pool.memset(keys[:, :, CMP_N:16], 0.0))
            step(pool.memset(cin[:, :, 0:TAPS - 1], 0.0))
            pool.memset(m_in[:, :, 0:ML_TAPS - 1], 0.0).then_inc(consts_ready, 1)

        @block.tensor
        def _(pe):
            pe.wait_ge(consts_ready, 1)
            pe.wait_ge(par_loaded, 16 * PAR_DMAS)
            pe.transpose(PS[:, 0, 0:PAR_ROWS], prow[0:PAR_ROWS, :], ident[0:PAR_ROWS, 0:PAR_ROWS])
            pe.transpose(PS[:, 1, 0:TAP_ROWS], trow[0:TAP_ROWS, :], ident[0:TAP_ROWS, 0:TAP_ROWS])\
                .then_inc(par_turned, 1)
            for f in range(8):
                if f >= 4:
                    pe.wait_ge(hT_ready, 2 * (f - 3))
                for k in (2 * f, 2 * f + 1):
                    for t in range(TT):
                        pe.wait_ge(hn_ready, t + 1)
                        mm = pe.transpose(PS[:, 4 + f % 4, (k % 2) * T + t * P:(k % 2) * T + (t + 1) * P],
                                          hn[:, t, k * P:(k + 1) * P], ident[:, :])
                mm.then_inc(h_turned, 1)

            pieces = {}

            def piece(f):
                pieces[f.__name__] = f
                return f

            @piece
            def forget_sum():
                pe.wait_ge(lf_ready, 1)
                pe.wait_ge(consts_ready, 2)
                pe.matmul(PS[:, 4, 0:4], upto[:, :], ml[:, 3, 0, :], start=True, stop=True)
                pe.matmul(PS[:, 4, 4:8], ones[:, :], ml[:, 3, 0, :], start=True, stop=False)
                pe.matmul(PS[:, 4, 4:8], upto[:, :], ml[:, 3, 1, :], start=False, stop=True).then_inc(f_summed, 1)

            @piece
            def ln_mean():
                pe.wait_ge(conv_step, TAPS * CT)
                for c in range(CT):
                    mm = pe.matmul(PS[:, 5, 0:T], av_ln, cacc[:, c, :], start=(c == 0), stop=(c == CT - 1))
                mm.then_inc(ln_sum, 1)

            @piece
            def ln_square():
                pe.wait_ge(ln_cen, 1)
                for c in range(CT):
                    mm = pe.matmul(PS[:, 6, 0:T], av_ln, tmp[:, c, :], start=(c == 0), stop=(c == CT - 1))
                mm.then_inc(ln_sq, 1)

            @piece
            def spread_gates():
                pe.wait_ge(diag_ready, 1)
                for t, b in ((0, 4), (1, 7)):
                    mm = pe.matmul(PS[:, b, :], ones[:, :], diag[:, t, :], start=True, stop=True)
                mm.then_inc(g_spread, 1)

            @piece
            def mlstm_scores():
                pe.wait_ge(mconv_out, 1)
                pe.wait_ge(gm_ready, 1)
                pe.wait_ge(ln_done, 1)
                for h in range(ML_H):
                    pe.matmul(PS[:, 4 + h, 0:P], mqk[:, h, 0:P], mqk[:, 4 + h, 0:P], start=True, stop=True)
                    pe.matmul(PS[:, 4 + h, P:3 * P], mqk[:, h, P:T], mqk[:, 4 + h, :], start=True, stop=True)\
                        .then_inc(qk_done, 1)

            @piece
            def mlstm_turn():
                for h in range(ML_H):
                    pe.wait_ge(s_ready, h + 1)
                    for i in range(3):
                        mm = pe.transpose(PS[:, 4 + h, i * P:(i + 1) * P], gmb[:, h, i, :], ident[:, :])
                    mm.then_inc(s_turned, 1)

            @piece
            def mlstm_values():
                for h in range(ML_H):
                    pe.wait_ge(sT_ready, h + 1)
                    s, v = pT[:, h % 2, :], slice(h * ML_D, (h + 1) * ML_D)
                    pe.matmul(PS[:, 4 + h, 0:P], s[:, 0:P], mv[:, 0, v], start=True, stop=True)
                    pe.matmul(PS[:, 4 + h, P:T], s[:, P:2 * P], mv[:, 0, v], start=True, stop=False)
                    pe.matmul(PS[:, 4 + h, P:T], s[:, 2 * P:3 * P], mv[:, 1, v], start=False, stop=True)\
                        .then_inc(num_done, 1)

            @piece
            def mlstm_columns():
                pe.wait_ge(hm_norm, 1)
                for h in range(ML_H):
                    for t in range(TT):
                        mm = pe.transpose(PS[:, 4 + h, t * P:(t + 1) * P], mo[:, t, h * ML_D:(h + 1) * ML_D],
                                          ident[:, :])
                    mm.then_inc(hm_turned, 1)

            @piece
            def hidden_columns():
                pe.wait_ge(unit_saved, units_with("w1v"))
                pe.wait_ge(s_ready, ML_H)
                for k in range(2):
                    mm = pe.transpose(PS[:, 4, k * P:(k + 1) * P], hid[:, k * P:(k + 1) * P], ident[:, :])
                mm.then_inc(hid_turned, 1)

            @piece
            def compressed():
                pe.wait_ge(hidT_ready, 1)
                pe.wait_ge(w2_loaded, 32)
                hT2 = hid[:, 256:512].rearrange("p (k n) -> p k n", k=2)
                for half in (0, 64):
                    for k in range(2):
                        pe.matmul(PS[half:half + 64, 5, 0:60], w2[:, 0, k, :], hT2[:, k, 0:60],
                                  start=(k == 0), stop=(k == 1))
                for g in range(GROUPS):
                    for k in range(2):
                        mm = pe.matmul(PS[0:CMP_N, 6, g * DH:(g + 1) * DH],
                                       hT2[:, k, 64 + g * CMP_N:64 + (g + 1) * CMP_N], w2[:, 1, k, :],
                                       start=(k == 0), stop=(k == 1))
                mm.then_inc(cmp_done, 1)

            def project(u):
                n, part, kind, s, i = UNITS[u]
                pe.wait_ge(w_loaded[n % RING], slab_at[n])
                if part == "small":
                    pe.wait_ge(small_loaded, 16)
                if part == "q":
                    pe.wait_ge(w_loaded[(n - 1) % RING], slab_at[n - 1])
                if kind == "hidden":
                    pe.wait_ge(blk_ready, 1)
                if u >= 4:
                    pe.wait_ge(unit_saved, u - 3 if u < LATE else max(u - 1, LATE))
                w = ring[:, n % RING, :, :]
                b = PS[:, unit_bank(u), :]
                for k in range(DK):
                    if kind == "rows":
                        cols = SMALL if part == "small" else 256
                        dst, lhs, rhs = b[:, 0:cols], hT[:, k, i * P:(i + 1) * P], w[:, k, 0:cols]
                    elif kind == "heads":
                        for g in range(2):
                            mm = pe.matmul(b[64 * g:64 * g + 64, 0:T],
                                           ring[:, n % RING - 1 + g, k, i * DH:(i + 1) * DH], hT[:, k, :],
                                           start=(k == 0), stop=(k == DK - 1))
                        continue
                    elif kind == "hidden":
                        r = 64 * (part == "w1v")
                        dst, lhs, rhs = b[r:r + 60, 0:256], blk[:, r // 64, k, :], w[:, k, :]
                    else:
                        dst, lhs, rhs = b[:, 0:T], w[:, k, i * P:(i + 1) * P], hT[:, k, :]
                    mm = pe.matmul(dst, lhs, rhs, start=(k == 0), stop=(k == DK - 1))
                mm.then_inc(unit_done, 1)

            pe.wait_ge(hT_ready, DK)
            for u in range(LATE):
                project(u)
                for piece in BETWEEN_PE.get(u, []):
                    pieces[piece]()

            pe.wait_ge(unit_saved, LATE)
            pe.wait_ge(cmp_saved, 1)
            tile, turn = [0], [0]

            def scores(a):
                p, g, t = ATT[a]
                rows = slice(64 * g, 64 * g + 64)
                for i in range(HPG):
                    for c0, c1 in ((0, 272), (272, 528))[:t + 1]:
                        if tile[0] >= 2:
                            pe.wait_ge(biased, tile[0] - 1)
                        pe.matmul(PS[:, 2 + tile[0] % 2, 0:c1 - c0], nsa_q[rows, 4 * p + i, t * P:(t + 1) * P],
                                  keys[rows, p, c0:c1], start=True, stop=True).then_inc(scored, 1)
                        tile[0] += 1

            def attend(a):
                p, g, t = ATT[a]
                G = 2 * p + g
                steps = [(0, k) for k in range(t + 1)] + [(1, k) for k in range(t + 1)] + [(2, 0)]
                o = PS[64 * g:64 * g + 64, 6 + a % 2, :]
                m0 = turn[0]
                pe.wait_ge(p_ready, a + 1)

                def turned(j):
                    br, k = steps[j]
                    m = m0 + j
                    if m >= 2:
                        pe.wait_ge(pT_ready, m - 1)
                    for i in range(HPG):
                        if br < 2:
                            mm = pe.transpose(PS[:, 4 + m % 2, i * P:(i + 1) * P],
                                              sc[:, a % 2, i, br, k * P:(k + 1) * P], ident[:, :])
                        else:
                            mm = pe.transpose(PS[0:16, 4 + m % 2, i * P:(i + 1) * P], sc_c[:, a % 2, i, :],
                                              ident[:, :])
                    mm.then_inc(p_turned, 1)

                turned(0)
                for j, (br, k) in enumerate(steps):
                    if j + 1 < len(steps):
                        turned(j + 1)
                    m = m0 + j
                    pe.wait_ge(pT_ready, m + 1)
                    if j == 0 and a >= 2:
                        pe.wait_ge(o_saved, a - 1)
                    lhs = vals[:, br, k, G * DH:(G + 1) * DH] if br < 2 else vcs[0:CMP_N, G, :]
                    rhs = pT[:, m % 2, :] if br < 2 else pT[0:CMP_N, m % 2, :]
                    pe.matmul(o, lhs, rhs, start=(j == 0), stop=(br == 2)).then_inc(pv_done, 1)
                turn[0] += len(steps)

            scores(0)
            for a in range(len(ATT)):
                if a + 1 < len(ATT):
                    scores(a + 1)
                project(LATE + a)
                attend(a)
            pe.wait_ge(o_saved, len(ATT))
            mlstm_turn()
            mlstm_values()
            pe.wait_ge(unit_saved, len(UNITS))
            for c in range(4):
                pe.wait_ge(osq_ready, c + 1)
                pe.matmul(PS[:, c, :], av_hd[:, :], osq[:, c * 512:(c + 1) * 512], start=True, stop=True)\
                    .then_inc(oms_done, 1)

            def out_part(v, features, first, last):
                m, t = v // TT, v % TT
                a, b = OUT_SLOTS[m]
                pe.wait_ge(w_loaded[a], out_at[m])
                for k in features:
                    if v == 0 and k < 8:
                        pe.wait_ge(attn_out, k + 1)
                    mm = pe.matmul(PS[:, v, :], mix[:, k, t * P:(t + 1) * P], ring[:, a:b + 1:b - a, k, :],
                                   start=(first and k == features[0]), stop=(last and k == features[-1]))
                if last:
                    mm.then_inc(out_done, 1)

            pe.wait_ge(conv_out, CT)
            pe.wait_ge(oroot, 4)
            for v in range(4):
                out_part(v, [12, 13, 14, 15] + list(range(8)), True, False)
            mlstm_columns()
            pe.wait_ge(hm_out, ML_H)
            for v in range(4):
                out_part(v, [8, 9, 10, 11], False, True)

            def turn_chunk(m):
                pe.wait_ge(out_added, TT * (m + 1))
                for f in range(2):
                    if m == 0:
                        pe.wait_ge(out_added, 4)
                    else:
                        pe.wait_ge(xnT_ready, 2 * m + f - 1)
                    for j in (2 * f, 2 * f + 1):
                        for t in range(TT):
                            mm = pe.transpose(PS[:, 2 + f, (j % 2) * T + t * P:(j % 2) * T + (t + 1) * P],
                                              x1[:, t, 512 * m + j:512 * (m + 1):4], ident[:, :])
                    mm.then_inc(xn_turned, 1)

            def route_chunk(m):
                pe.wait_ge(xnT_ready, 2 * (m + 1))
                for k in range(4 * m, 4 * m + 4):
                    for t in range(TT):
                        mm = pe.matmul(PS[:, t, 0:EG + E], xnT[:, k, t * P:(t + 1) * P], roww[:, k, :],
                                       start=(k == 0), stop=(k == DK - 1))
                return mm

            everything = list(range(DK))
            out_part(4, everything, True, True)
            out_part(5, everything, True, True)
            pe.wait_ge(roww_ready, 1)
            turn_chunk(0)
            turn_chunk(1)
            out_part(6, everything, True, True)
            route_chunk(0)
            turn_chunk(2)
            out_part(7, everything, True, True)
            route_chunk(1)
            route_chunk(2)
            turn_chunk(3)
            route_chunk(3).then_inc(logits_done, 1)
            pe.wait_ge(picks_ready, 1)
            A = ro[:, 0, :, :]
            pe.matmul(PS[:, 5, 0:E], before[:, :], A[:, 0, :], start=True, stop=True)
            pe.matmul(PS[:, 5, 64:64 + E], ones[:, :], A[:, 0, :], start=True, stop=False)
            pe.matmul(PS[:, 5, 64:64 + E], before[:, :], A[:, 1, :], start=False, stop=True)
            pe.matmul(PS[0:E, 6, 0:1], A[:, 0, :], ones[:, 0:1], start=True, stop=False)
            pe.matmul(PS[0:E, 6, 0:1], A[:, 1, :], ones[:, 0:1], start=False, stop=True).then_inc(ranks_done, 1)
            pe.wait_ge(blocks_step, 3)
            pe.matmul(PS[0:E, 7, 0:1], before[0:E, 0:E], ovt[:, 1:2], start=True, stop=True).then_inc(blocks_pe, 1)
            pe.wait_ge(blocks_step, 10)
            pe.matmul(PS[:, 6, 64:64 + 3 * BLOCKS], ones[0:E, :], own[:, :, :].rearrange("e a b -> e (a b)"),
                      start=True, stop=True).then_inc(blocks_pe, 1)

            def gather(n, w0, width, saved0):
                for f in range(8):
                    if f >= 2:
                        pe.wait_ge(n, saved0 + (f - 1))
                    for k in (2 * f, 2 * f + 1):
                        for t in range(TT):
                            mm = pe.matmul(PS[:, 6 + f % 2, (k % 2) * 256:(k % 2) * 256 + width],
                                           xn[:, t, k, :], sel[:, t, :, :].rearrange("p a b -> p (a b)")[:, 0:width],
                                           start=(t == 0), stop=(t == TT - 1))
                    mm.then_inc(g_filled, 1)

            def gate_up(i, c):
                w = ring_flat[:, CHUNK_SLOT[c], :].rearrange("p (u j n) -> p u j n", u=2, j=4)
                for j in range(4):
                    for u in range(2):
                        mm = pe.matmul(PS[64 * u:64 * u + 64, 0, :], XG[:, 4 * c + j, i * SLOTS:(i + 1) * SLOTS],
                                       w[:, u, j, :], start=(c == 0 and j == 0), stop=(c == 3 and j == 3))
                return mm

            def hidden_turn():
                for k in range(4):
                    mm = pe.transpose(PS[:, 1, k * P:(k + 1) * P], Hs[:, k * P:(k + 1) * P], ident[:, :])
                return mm

            def down(c):
                w = ring_flat[:, CHUNK_SLOT[c], :].rearrange("p (j n) -> p j n", j=2)
                for j in range(2):
                    k = 2 * (c - 4) + j
                    for b in range(2):
                        for half in range(2):
                            mm = pe.matmul(PS[64 * half:64 * half + 64, 2 + b, :], hTe[:, k, :],
                                           w[:, j, half * 1024 + b * 512:half * 1024 + (b + 1) * 512],
                                           start=(k == 0), stop=(k == 3))
                return mm

            def scatter(pair, t, cols, rows=P):
                for b in range(2):
                    mm = pe.matmul(PS[:, 4 + b, :], SW[0:rows, pair, t * P:(t + 1) * P],
                                   Y2[0:rows, pair, (2 * cols + b) * 512:(2 * cols + b + 1) * 512],
                                   start=True, stop=True)
                mm.then_inc(sc_filled, 1)

            def turn_weights(rows, pairs):
                for pair in range(pairs):
                    for t in range(TT):
                        mm = pe.transpose(
                            PS[0:rows, 6, pair * T + t * P:pair * T + (t + 1) * P],
                            selw[:, t, :, :].rearrange("p a b -> p (a b)")[:, pair * P:pair * P + rows], ident[:, :])
                mm.then_inc(sw_filled, 1)

            pe.wait_ge(zeroed, 1)
            pe.wait_ge(blocks_ready, 2)
            with pe.Fori(0, NQUAD) as q:
                pe.wait_ge(sel_ready, q + 1)
                gather(g_saved, 0, QUAD * SLOTS, q * 8)
                pe.wait_ge(g_saved, q * 8 + 8)
                for i in range(QUAD):
                    for c in range(4):
                        pe.wait_ge(w_loaded[CHUNK_SLOT[c]],
                                   q * (QUAD * CHUNK_INC[c]) + ((i + 1) * CHUNK_INC[c] + slot_total[CHUNK_SLOT[c]]))
                        gate_up(i, c).then_inc(w_used[c], 1)
                    pair, t = (i // 2 + 1) % 2, i % 2
                    if t == 0:
                        pe.wait_ge(y_saved_a, q * QUAD + (i + 1))
                        pe.wait_ge(y_saved_d, q * QUAD + (i + 1))
                    pe.wait_ge(sc_added, q * 8 + (2 * i + 1))
                    scatter(pair, t, 0)
                    pe.wait_ge(h_saved, q * QUAD + (i + 1))
                    hidden_turn().then_inc(h_turned_e, 1)
                    pe.wait_ge(sc_added, q * 8 + (2 * i + 2))
                    scatter(pair, t, 1)
                    pe.wait_ge(hid_ready, q * QUAD + (i + 2))
                    pe.wait_ge(y_saved_a, q * QUAD + (i + 1))
                    pe.wait_ge(y_saved_d, q * QUAD + (i + 1))
                    for c in range(4, 6):
                        pe.wait_ge(w_loaded[CHUNK_SLOT[c]],
                                   q * (QUAD * CHUNK_INC[c]) + ((i + 1) * CHUNK_INC[c] + slot_total[CHUNK_SLOT[c]]))
                        down(c).then_inc(w_used[c], 1)
                    if i == 1:
                        turn_weights(P, 2)
                        pe.wait_ge(sw_saved, q + 1)
            pe.wait_ge(y_saved_a, E + 1)
            pe.wait_ge(y_saved_d, E + 1)
            for t in range(TT):
                for cols in range(2):
                    pe.wait_ge(sc_added, 8 * NQUAD + 2 * t + cols + 1)
                    scatter(1, t, cols)

            with pe.Fori(0, BLOCKS) as b:
                active = pe.value_load(blk_i[0:1, bass.ds(b + 2 * BLOCKS, 1)], min_val=0, max_val=1)
                with pe.If(active > 0):
                    pe.wait_ge(ov_sel, b + 1)
                    for f in range(8):
                        if f >= 2:
                            pe.wait_ge(ov_act, b * OV_ACT + (f - 1))
                        for k in (2 * f, 2 * f + 1):
                            for t in range(TT):
                                mm = pe.matmul(PS[:, 6 + f % 2, (k % 2) * 256:(k % 2) * 256 + SLOTS],
                                               xn[:, t, k, :], sel[:, t, 0, :], start=(t == 0), stop=(t == TT - 1))
                        mm.then_inc(ov_pe, 1)
                    for t in range(TT):
                        if t == 0:
                            pe.wait_ge(ov_act, b * OV_ACT + 7)
                        mm = pe.transpose(PS[:, 6, t * P:(t + 1) * P],
                                          selw[:, t, 0:2, :].rearrange("p a b -> p (a b)"), ident[:, :])
                    mm.then_inc(ov_pe, 1)
                    pe.wait_ge(ov_act, b * OV_ACT + 8)
                    for c in range(4):
                        pe.wait_ge(ov_loaded[c], b * CHUNK_INC[c] + CHUNK_INC[c])
                        mm = gate_up(0, c)
                    mm.then_inc(ov_pe, 1)
                    pe.wait_ge(ov_act, b * OV_ACT + 10)
                    hidden_turn().then_inc(ov_pe, 1)
                    pe.wait_ge(ov_dve, b * OV_DVE + 1)
                    for c in range(4, 6):
                        pe.wait_ge(ov_loaded[c], b * CHUNK_INC[c] + CHUNK_INC[c])
                        mm = down(c)
                    mm.then_inc(ov_pe, 1)
                    pe.wait_ge(ov_act, b * OV_ACT + 13)
                    for i in range(4):
                        t, cols = i // 2, i % 2
                        if i >= 2:
                            pe.wait_ge(ov_dve, b * OV_DVE + i)
                        for c in range(2):
                            mm = pe.matmul(PS[:, OV_BANK[i] + c, :], SW[0:SLOTS, 0, t * P:(t + 1) * P],
                                           Y2[0:SLOTS, 0, (2 * cols + c) * 512:(2 * cols + c + 1) * 512],
                                           start=True, stop=True)
                        mm.then_inc(ov_pe, 1)
                    pe.wait_ge(ov_end, b + 1)
                    pe.sem_inc(ov_left, 1)
                with pe.Else():
                    pe.sem_inc(ov_pe, OV_PE)

        @block.scalar
        def _(act):
            def load_rows(dst, src, done=par_loaded):
                act.dma_start(dst, src).then_inc(done, 16)

            def at(name, n):
                return prow[PAR[name]:PAR[name] + n, :]

            load_rows(at("attn_g", 16), attn_norm_g[0].rearrange("(r c) -> r c", c=P))
            heads_g = nsa_out_g[0].rearrange("(p g i d) -> p g i d", p=2, g=2, i=HPG)
            for p in range(2):
                for g in range(2):
                    r = PAR["nsa_g"] + 4 * p
                    load_rows(prow[r:r + 4, 64 * g:64 * g + 64], heads_g[p, g])
            load_rows(at("ml_g", 4), mlstm_out_g[0].rearrange("(r c) -> r c", c=P))
            load_rows(at("mconv_w", 32), mlstm_conv_w[0].rearrange("k (r c) -> (k r) c", c=P))
            load_rows(at("mconv_b", 8), mlstm_conv_b[0].rearrange("(r c) -> r c", c=P))
            load_rows(at("conv_b", 4), conv_b[0].rearrange("(r c) -> r c", c=P))
            load_rows(at("ln_g", 4), conv_ln_g[0].rearrange("(r c) -> r c", c=P))
            load_rows(at("ln_b", 4), conv_ln_b[0].rearrange("(r c) -> r c", c=P))
            load_rows(at("pos_k", 16), cmp_pos_k[0].rearrange("(r l) d -> r (l d)", l=2))
            load_rows(at("pos_v", 16), cmp_pos_v[0].rearrange("(r l) d -> r (l d)", l=2))
            load_rows(trow[0:TAP_ROWS, :], conv_w[0].rearrange("k (r c) -> (k r) c", c=P))

            act_n = [0]

            def step(ins):
                act_n[0] += 1
                ins.then_inc(act_step, 1)
                act.wait_ge(act_step, act_n[0])

            act.wait_ge(consts_ready, 1)
            act.wait_ge(x_loaded, 16 * TT)
            for t in range(TT):
                step(act.activation(hn[:, t, :], x1[:, t, :], ACT.Square, bias=ZERO_C, accum_out=st[:, t:t + 1]))
            act.activation(st[:, 2:4], st[:, 0:2], ACT.Sqrt, bias=EPS_C, scale=1.0 / D).then_inc(rstd_root, 1)
            load_rows(w2[:, 0, :, :], cmp_w2_k[0].rearrange("(k p) n -> p k n", p=P), w2_loaded)
            load_rows(w2[:, 1, :, :], cmp_w2_v[0].rearrange("(k p) n -> p k n", p=P), w2_loaded)
            load_rows(fi_b[:, 0:4], mlstm_i_bias[0].partition_broadcast(P), bias_loaded)
            load_rows(fi_b[:, 4:8], mlstm_f_bias[0].partition_broadcast(P), bias_loaded)
            load_rows(rout_b[:, 0:EG], router_b_group[0].partition_broadcast(P), router_loaded)
            load_rows(rout_b[:, EG:EG + E], router_b_expert[0].rearrange("g e -> (g e)").partition_broadcast(P),
                      router_loaded)
            rg = router_w_group[0].rearrange("(c p j) n -> c p j n", c=4, j=4)
            re = router_w_expert[0].rearrange("(c p j) n -> c p j n", c=4, j=4)
            load_rows(ffn_gc[:, :, :], ffn_norm_g[0].rearrange("(c p j) -> p c j", c=4, j=4), router_loaded)
            for c in range(4):
                load_rows(roww[:, 4 * c:4 * c + 4, 0:EG], rg[c], router_loaded)
                load_rows(roww[:, 4 * c:4 * c + 4, EG:EG + E], re[c], router_loaded)

            pieces = {}

            def piece(f):
                pieces[f.__name__] = f
                return f

            @piece
            def conv_silu():
                act.wait_ge(mconv_step, 8 * ML_TAPS)
                act.activation(mqk, mqk, ACT.Silu, bias=ZERO_C).then_inc(mconv_out, 1)

            @piece
            def forget_logs():
                act.wait_ge(f_in, 1)
                act.activation(ml[:, 1, :, :], ml[:, 0, :, :], ACT.Exp, bias=ZERO_C).then_inc(lf_exp, 1)
                act.wait_ge(lf_exp, 1)
                act.activation(ml[:, 2, :, :], ml[:, 1, :, :], ACT.Ln, bias=ONE_C).then_inc(lf_log, 1)

            @piece
            def ln_std():
                act.wait_ge(ln_sq, 1)
                act.activation(pT[:, 0, 0:T], PS[:, 6, 0:T], ACT.Sqrt, bias=LN_EPS_C).then_inc(ln_root, 1)

            @piece
            def conv_result():
                act.wait_ge(ln_done, 1)
                for c in range(CT):
                    act.activation(cacc[:, c, :], cacc[:, c, :], ACT.Silu, bias=par[:, PAR["ln_b"] + c:PAR["ln_b"] + c + 1],
                                   scale=par[:, PAR["ln_g"] + c:PAR["ln_g"] + c + 1]).then_inc(conv_out, 1)

            @piece
            def decays():
                act.wait_ge(gm_ready, 1)
                for h in range(ML_H):
                    act.activation(gmb[:, h, 0, :], gmb[:, h, 0, :], ACT.Exp, bias=ml[:, 7, 0, h:h + 1])\
                        .then_inc(decay_ready, 1)
                    act.activation(gmb[:, h, 1:3, :], gmb[:, h, 1:3, :], ACT.Exp, bias=ml[:, 7, 1, h:h + 1])\
                        .then_inc(decay_ready, 1)
                act.activation(ml[:, 8, :, :], ml[:, 9, :, :], ACT.Exp, bias=ZERO_C).then_inc(decay_ready, 1)

            @piece
            def mlstm_saves():
                for h in range(ML_H):
                    act.wait_ge(s_turned, h + 1)
                    if h >= 2:
                        act.wait_ge(num_done, h - 1)
                    act.activation(pT[:, h % 2, 0:3 * P], PS[:, 4 + h, 0:3 * P], ACT.Copy).then_inc(sT_ready, 1)

            @piece
            def mlstm_root():
                act.wait_ge(hm_sq, 1)
                act.activation(ml[:, 11, :, :], ml[:, 10, :, :], ACT.Sqrt, bias=EPS_C, scale=1.0 / ML_D)\
                    .then_inc(hm_root, 1)

            @piece
            def mlstm_result():
                for h in range(ML_H):
                    act.wait_ge(hm_turned, h + 1)
                    act.activation(mix[:, 8 + h, :], PS[:, 4 + h, 0:T], ACT.Copy,
                                   scale=par[:, PAR["ml_g"] + h:PAR["ml_g"] + h + 1]).then_inc(hm_out, 1)

            @piece
            def hidden_save():
                act.wait_ge(hid_turned, 1)
                act.activation(hid[:, 256:512], PS[:, 4, 0:256], ACT.Copy).then_inc(hidT_ready, 1)

            @piece
            def compressed_save():
                act.wait_ge(cmp_done, 1)
                for half in range(2):
                    src = PS[64 * half:64 * half + 64, 5, 0:60].rearrange("d (p g n) -> d p g n", p=2, g=2)
                    step(act.activation(keys[64 * half:64 * half + 64, :, 0:CMP_N], src[:, :, half, :], ACT.Copy))
                act.activation(vcs[0:CMP_N, :, :], PS[0:CMP_N, 6, 0:256].rearrange("n (g d) -> n g d", g=GROUPS),
                               ACT.Copy).then_inc(cmp_saved, 1)

            def save_unit(u):
                n, part, kind, s, i = UNITS[u]
                b = PS[:, unit_bank(u), 0:256]
                f, scale, c = ACT.Copy, 1.0, 2 * s + i
                if part == "cg":
                    dst, f = cgs[:, c, :], ACT.Sigmoid
                elif part == "ca":
                    dst = cin[:, c, TAPS - 1:]
                elif part in ("mq", "mk"):
                    dst = m_in[:, c + 4 * (part == "mk"), ML_TAPS - 1:]
                elif part == "small":
                    b = b[:, 0:SMALL]
                    step(act.activation(gates[:, i, 0:48], b[:, 0:48], ACT.Sigmoid, bias=ZERO_C))
                    return act.activation(gates[:, i, 48:56], b[:, 48:56], ACT.Copy)
                elif part == "mv":
                    dst = mv[:, i, s * 256:(s + 1) * 256]
                elif part == "mo":
                    dst, f = mo[:, i, s * 256:(s + 1) * 256], ACT.Sigmoid
                elif part in ("kc", "vc"):
                    dst = kcv[:, i + 2 * (part == "vc"), :]
                elif part in ("ks", "kw"):
                    c0 = 16 + P * (part == "kw")
                    dst = keys[:, i, c0:c0 + 384].rearrange("d (t k) -> d t k", k=P)[:, ::2, :]
                    b = b.rearrange("d (t k) -> d t k", t=TT)
                elif part in ("vs", "vw"):
                    dst = vals[:, int(part == "vw"), i, :]
                elif part == "q":
                    dst, scale = nsa_q[:, 4 * s + i, :], DH ** -0.5
                else:
                    r = 64 * (part == "w1v")
                    dst, b, f = hid[r:r + 60, 0:256], b[r:r + 60], ACT.Silu
                if f == ACT.Copy:
                    return act.activation(dst, b, f, scale=scale)
                return act.activation(dst, b, f, bias=ZERO_C[0:b.shape[0]] if part != "w1v" else small_c[64:124, 3:4])

            for u in range(LATE):
                if u == units_before("q"):
                    act.wait_ge(g_spread, 1)
                act.wait_ge(unit_done, u + 1)
                save_unit(u).then_inc(unit_saved, 1)
                for name in BETWEEN_ACT.get(u, []):
                    pieces[name]()

            turn = [0]

            def exponents(a):
                p, g, t = ATT[a]
                act.wait_ge(max_ready, a + 1)
                u, w = a % 2, P * (t + 1)
                for i in range(HPG):
                    for br in range(2):
                        s = sc[:, u, i, br, 0:w]
                        act.activation(s, s, ACT.Exp, bias=rs[:, u, 0, i, 1 + br:2 + br],
                                       accum_out=rs[:, u, 1, i, 1 + br:2 + br])
                    s = sc_c[:, u, i, :]
                    e = act.activation(s, s, ACT.Exp, bias=rs[:, u, 0, i, 0:1], accum_out=rs[:, u, 1, i, 0:1])
                e.then_inc(exp_done, 1)

            def attend_saves(a):
                p, g, t = ATT[a]
                n = 2 * (t + 1) + 1
                for j in range(n):
                    m = turn[0] + j
                    act.wait_ge(p_turned, m + 1)
                    if m >= 2:
                        act.wait_ge(pv_done, m - 1)
                    rows = P if j < n - 1 else 16
                    act.activation(pT[0:rows, m % 2, :], PS[0:rows, 4 + m % 2, :], ACT.Copy).then_inc(pT_ready, 1)
                turn[0] += n
                act.wait_ge(pv_done, turn[0])
                rows = slice(64 * g, 64 * g + 64)
                act.activation(mix[rows, 4 * p:4 * p + 4, t * P:(t + 1) * P],
                               PS[rows, 6 + a % 2, :].rearrange("d (i q) -> d i q", i=HPG), ACT.Copy)\
                    .then_inc(o_saved, 1)

            exponents(0)
            for a in range(len(ATT)):
                if a + 1 < len(ATT):
                    exponents(a + 1)
                act.wait_ge(unit_done, LATE + a + 1)
                save_unit(LATE + a).then_inc(unit_saved, 1)
                attend_saves(a)
            mlstm_saves()
            mlstm_root()
            for c in range(4):
                act.wait_ge(oms_done, c + 1)
                act.activation(oroot_b[:, c * 512:(c + 1) * 512], PS[:, c, :], ACT.Sqrt, bias=EPS_C)\
                    .then_inc(oroot, 1)
            mlstm_result()
            load_rows(fin_g[:, :], ffn_norm_g[0].partition_broadcast(P), gain_loaded)

            def copy_chunk(m):
                for f in range(2 * m, 2 * m + 2):
                    act.wait_ge(xn_turned, f + 1)
                    act.activation(xnT[:, 2 * f:2 * f + 2, :], PS[:, 2 + f % 2, :].rearrange("p (k n) -> p k n", k=2),
                                   ACT.Copy).then_inc(xnT_ready, 1)

            act.wait_ge(attn_out, 8)
            for v in range(4 * TT):
                if v == 6:
                    copy_chunk(0)
                    copy_chunk(1)
                if v == 7:
                    copy_chunk(2)
                m, t = v // TT, v % TT
                act.wait_ge(out_added, v + 1)
                act.activation(att[:, v * 512:(v + 1) * 512], x1[:, t, m * 512:(m + 1) * 512], ACT.Square,
                               bias=ZERO_C, accum_out=ssq[:, t, m:m + 1]).then_inc(ffn_ssq, 1)
            act.wait_ge(ffn_summed, 1)
            act.activation(st[:, 8:10], st[:, 6:8], ACT.Sqrt, bias=EPS_C, scale=1.0 / D).then_inc(ffn_root, 1)
            copy_chunk(3)
            act.wait_ge(route_max, 1)
            act.activation(rt[:, 10, :], rt[:, 9, :], ACT.Exp, bias=ZERO_C).then_inc(route_exp, 1)
            act.activation(ro[:, 7, :, 0:EG], ro[:, 6, :, 0:EG], ACT.Exp, bias=ZERO_C).then_inc(route_exp, 1)
            act.wait_ge(xn_ready, TT)
            load_rows(fin_g[:, :], final_norm_g.partition_broadcast(P), fing_loaded)

            def save_gather(f, width):
                act.activation(XG[:, 2 * f:2 * f + 2, 0:width],
                               PS[:, 6 + f % 2, :].rearrange("p (k n) -> p k n", k=2)[:, :, 0:width],
                               ACT.Copy).then_inc(g_saved if width > SLOTS else ov_act, 1)

            HT = PS[:, 1, :].rearrange("p (k n) -> p k n", k=4)
            act.wait_ge(blocks_ready, 2)
            act.sem_inc(y_saved_a, 1)
            with act.Fori(0, NQUAD) as q:
                for f in range(8):
                    act.wait_ge(g_filled, q * 8 + (f + 1))
                    save_gather(f, QUAD * SLOTS)
                for i in range(QUAD):
                    act.wait_ge(w_used[3], q * QUAD + (i + 1))
                    act.activation(Hs[:, :], PS[:, 0, :], ACT.Copy).then_inc(h_saved, 1)
                    act.wait_ge(h_turned_e, q * QUAD + (i + 1))
                    act.wait_ge(hid_ready, q * QUAD + (i + 1))
                    act.activation(sg[:, :, :], HT[:, :, 0:SLOTS], ACT.Silu, bias=ZERO_C).then_inc(silu_done, 1)
                    act.wait_ge(w_used[5], q * QUAD + (i + 1))
                    r = 64 * (i % 2)
                    act.activation(Y2[r:r + 64, i // 2, 0:1024],
                                   PS[0:64, 2:4, :].rearrange("p a b -> p (a b)"), ACT.Copy).then_inc(y_saved_a, 1)
                    if i == 1:
                        act.wait_ge(sw_filled, q + 1)
                        act.activation(SW[:, :, :], PS[:, 6, :].rearrange("p (a b) -> p a b", a=2), ACT.Copy)\
                            .then_inc(sw_saved, 1)

            with act.Fori(0, BLOCKS) as b:
                active = act.value_load(blk_i[0:1, bass.ds(b + 2 * BLOCKS, 1)], min_val=0, max_val=1)
                with act.If(active > 0):
                    for f in range(8):
                        act.wait_ge(ov_pe, b * OV_PE + (f + 1))
                        save_gather(f, SLOTS)
                    act.wait_ge(ov_pe, b * OV_PE + 9)
                    act.activation(SW[0:64, 0, :], PS[0:64, 6, 0:T], ACT.Copy).then_inc(ov_act, 1)
                    act.wait_ge(ov_pe, b * OV_PE + 10)
                    act.activation(Hs[:, :], PS[:, 0, :], ACT.Copy).then_inc(ov_act, 1)
                    act.wait_ge(ov_pe, b * OV_PE + 11)
                    act.activation(sg[:, :, :], HT[:, :, 0:SLOTS], ACT.Silu, bias=ZERO_C).then_inc(ov_act, 1)
                    act.wait_ge(ov_pe, b * OV_PE + 12)
                    for half in range(2):
                        act.activation(Y2[0:64, 0, 1024 * half:1024 * (half + 1)],
                                       PS[64 * half:64 * half + 64, 2:4, :].rearrange("p a b -> p (a b)"),
                                       ACT.Copy).then_inc(ov_act, 1)
                    act.wait_ge(ov_end, b + 1)
                    act.sem_inc(ov_left, 1)
                with act.Else():
                    act.sem_inc(ov_act, OV_ACT)
            act.wait_ge(ov_end, BLOCKS)
            for t in range(TT):
                step(act.activation(Y2[:, t, :], x1[:, t, :], ACT.Square, bias=ZERO_C,
                                    accum_out=st[:, 10 + t:11 + t]))
            act.activation(st[:, 12:14], st[:, 10:12], ACT.Sqrt, bias=EPS_C, scale=1.0 / D).then_inc(fin_root, 1)

        @block.vector
        def _(dve):
            dve_n = [0]

            def step(ins):
                dve_n[0] += 1
                ins.then_inc(dve_step, 1)
                dve.wait_ge(dve_step, dve_n[0])

            def col(name, i):
                return par[:, PAR[name] + i:PAR[name] + i + 1]

            dve.wait_ge(par_turned, 1)
            step(dve.tensor_copy(par[:, :], PS[:, 0, 0:PAR_ROWS]))
            step(dve.tensor_copy(taps[:, :], PS[:, 1, 0:TAP_ROWS]))
            dve.wait_ge(rstd_root, 1)
            step(dve.reciprocal(st[:, 4:6], st[:, 2:4]))
            for t in range(TT):
                dve.tensor_scalar(hn[:, t, :], x1[:, t, :], st[:, 4 + t:5 + t], None, ALU.mult).then_inc(hn_ready, 1)
            for k in range(DK):
                dve.wait_ge(h_turned, k // 2 + 1)
                dve.tensor_scalar(hT[:, k, :], PS[:, 4 + (k // 2) % 4, (k % 2) * T:(k % 2 + 1) * T],
                                  col("attn_g", k), None, ALU.mult).then_inc(hT_ready, 1)

            dve.wait_ge(unit_saved, units_with("ca"))
            dve.wait_ge(consts_ready, 2)
            step(dve.tensor_tensor(cin[:, :, TAPS - 1:], cin[:, :, TAPS - 1:], cgs, ALU.mult))
            for j in range(TAPS):
                for c in range(CT):
                    src, w = cin[:, c, j:j + T], taps[:, j * CT + c:j * CT + c + 1]
                    if j == 0:
                        ins = dve.tensor_scalar(cacc[:, c, :], src, w, col("conv_b", c), ALU.mult, ALU.add)
                    else:
                        dve.wait_ge(conv_step, CT * (j - 1) + c + 1)
                        ins = dve.scalar_tensor_tensor(out=cacc[:, c, :], in0=src, scalar=w, in1=cacc[:, c, :],
                                                       op0=ALU.mult, op1=ALU.add)
                    ins.then_inc(conv_step, 1)
            dve.wait_ge(unit_saved, units_with("mk"))
            for j in range(ML_TAPS):
                for c in range(8):
                    src = m_in[:, c, j:j + T]
                    w = col("mconv_w", 8 * j + c)
                    if j == 0:
                        ins = dve.tensor_scalar(mqk[:, c, :], src, w, col("mconv_b", c), ALU.mult, ALU.add)
                    else:
                        dve.wait_ge(mconv_step, 8 * (j - 1) + c + 1)
                        ins = dve.scalar_tensor_tensor(out=mqk[:, c, :], in0=src, scalar=w, in1=mqk[:, c, :],
                                                       op0=ALU.mult, op1=ALU.add)
                    ins.then_inc(mconv_step, 1)
            dve.wait_ge(unit_saved, units_with("small"))
            dve.wait_ge(bias_loaded, 32)
            fi = gates[:, :, 48:56]
            step(dve.tensor_tensor(fi, fi, fi_b[:, :].unsqueeze(1).broadcast_to([P, TT, 8]), ALU.add))
            ig, fg = gates[:, :, 48:52], gates[:, :, 52:56]
            dve.scalar_tensor_tensor(out=ml[:, 0, :, :], in0=fg, scalar=-1.0, in1=fg, op0=ALU.mult, op1=ALU.min)\
                .then_inc(f_in, 1)
            dve.wait_ge(lf_log, 1)
            dve.scalar_tensor_tensor(out=ml[:, 3, :, :], in0=fg, scalar=0.0, in1=ml[:, 2, :, :], op0=ALU.min,
                                     op1=ALU.subtract).then_inc(lf_ready, 1)
            dve.wait_ge(conv_step, TAPS * CT)
            dve.wait_ge(ln_sum, 1)
            step(dve.tensor_tensor(cacc, cacc, PS[:, 5, 0:T].unsqueeze(1).broadcast_to([P, CT, T]), ALU.subtract))
            dve.tensor_tensor(tmp, cacc, cacc, ALU.mult).then_inc(ln_cen, 1)
            dve.wait_ge(ln_root, 1)
            step(dve.reciprocal(pT[:, 0, 0:T], pT[:, 0, 0:T]))
            dve.tensor_tensor(cacc, cacc, pT[:, 0:1, 0:T].broadcast_to([P, CT, T]), ALU.mult).then_inc(ln_done, 1)
            dve.wait_ge(f_summed, 1)
            B = ml[:, 4, :, :]
            step(dve.tensor_copy(B, PS[:, 4, 0:8].rearrange("p (t h) -> p t h", t=TT)))
            step(dve.tensor_tensor(ml[:, 5, :, :], ig, B, ALU.subtract))
            for t in range(TT):
                ins = dve.tensor_tensor(diag[:, t, :].rearrange("p (h s) -> p h s", h=ML_H),
                                        ident[:, :].unsqueeze(1).broadcast_to([P, ML_H, P]),
                                        ml[:, 5, t, :].unsqueeze(2).broadcast_to([P, ML_H, P]), ALU.mult)
                if t == 0:
                    step(ins)
                else:
                    ins.then_inc(diag_ready, 1)
            dve.wait_ge(mconv_step, 8 * ML_TAPS)
            dve.wait_ge(unit_saved, units_with("vc"))
            for b in range(2):
                for g in range(GROUPS):
                    for half in range(2):
                        r = 64 * (g % 2)
                        base = kcv[r:r + 64, 2 * b + g // 2, :]
                        src = bass.AP(base.tensor, base.offset + half, [list(base.ap[0]), [2, CMP_J], [16, CMP_N]])
                        step(dve.tensor_copy(blk[64 * half:64 * half + 64, b, :, g * CMP_N:(g + 1) * CMP_N], src))
            for b, name in enumerate(("pos_k", "pos_v")):
                pos = par[:, PAR[name]:PAR[name] + CMP_J].unsqueeze(2).broadcast_to([P, CMP_J, 60])
                ins = dve.tensor_tensor(blk[:, b, :, :], blk[:, b, :, :], pos, ALU.add)
                if b == 0:
                    step(ins)
                else:
                    ins.then_inc(blk_ready, 1)
            dve.wait_ge(g_spread, 1)
            spread = [PS[:, b, :].rearrange("p (h s) -> p h s", h=ML_H) for b in (4, 7)]
            mask_h = cmask[:, :].unsqueeze(1).broadcast_to([P, ML_H, P])
            step(dve.tensor_tensor(gmb[:, :, 0, :], spread[0], mask_h, ALU.add))
            step(dve.tensor_copy(gmb[:, :, 1, :], spread[0]))
            step(dve.tensor_tensor(gmb[:, :, 2, :], spread[1], mask_h, ALU.add))
            step(dve.tensor_reduce(ml[:, 6, 0, :], gmb[:, :, 0, :], AX, ALU.max))
            step(dve.tensor_reduce(ml[:, 6, 1, :], gmb[:, :, 1:3, :].rearrange("p h a b -> p h (a b)"), AX, ALU.max))
            step(dve.tensor_scalar(ml[:, 7, :, :], ml[:, 6, :, :], 0.0, -1.0, ALU.max, ALU.mult))
            dve.tensor_tensor(ml[:, 9, :, :], ml[:, 7, :, :], B, ALU.subtract).then_inc(gm_ready, 1)
            for h in range(ML_H):
                dve.wait_ge(qk_done, h + 1)
                dve.wait_ge(decay_ready, 2 * (h + 1))
                flat = gmb[:, h, :, :].rearrange("p a b -> p (a b)")
                dve.scalar_tensor_tensor(out=flat, in0=PS[:, 4 + h, 0:3 * P], scalar=ML_D ** -0.5, in1=flat,
                                         op0=ALU.mult, op1=ALU.mult).then_inc(s_ready, 1)
            dve.wait_ge(s_ready, ML_H)
            step(dve.tensor_reduce(ml[:, 6, 0, :], gmb[:, :, 0, :], AX, ALU.add))
            step(dve.tensor_reduce(ml[:, 6, 1, :], gmb[:, :, 1:3, :].rearrange("p h a b -> p h (a b)"), AX, ALU.add))
            step(dve.tensor_scalar(ml[:, 7, :, :], ml[:, 6, :, :], -1.0, None, ALU.mult))
            step(dve.tensor_tensor(ml[:, 6, :, :], ml[:, 6, :, :], ml[:, 7, :, :], ALU.max))
            dve.wait_ge(decay_ready, 2 * ML_H + 1)
            step(dve.tensor_tensor(ml[:, 6, :, :], ml[:, 6, :, :], ml[:, 8, :, :], ALU.max))
            step(dve.reciprocal(ml[:, 7, :, :], ml[:, 6, :, :]))
            mo_v = mo[:, :, :].rearrange("p t (h d) -> p t h d", h=ML_H)

            tile = [0]
            turned = [sum(2 * (ATT[b][2] + 1) + 1 for b in range(a)) for a in range(len(ATT) + 1)]

            def biases(a):
                p, g, t = ATT[a]
                u = a % 2
                if a >= 2:
                    dve.wait_ge(p_turned, turned[a - 1])
                for i in range(HPG):
                    slope = SLOPES[(2 * p + g) * HPG + i]
                    for part in range(t + 1):
                        b = PS[:, 2 + tile[0] % 2, :]
                        dve.wait_ge(scored, tile[0] + 1)
                        off = 16 * (part == 0)
                        d = dist[:, 1 if part == t else 0, :].unsqueeze(1).broadcast_to([P, 2, P])
                        if part == 0:
                            dve.scalar_tensor_tensor(out=sc_c[:, u, i, :], in0=dist_c[:, t, :], scalar=slope,
                                                     in1=b[:, 0:16], op0=ALU.mult, op1=ALU.add)
                        dve.scalar_tensor_tensor(out=sc[:, u, i, :, part * P:(part + 1) * P], in0=d, scalar=slope,
                                                 in1=b[:, off:off + 256].rearrange("p (a b) -> p a b", a=2),
                                                 op0=ALU.mult, op1=ALU.add).then_inc(biased, 1)
                        tile[0] += 1
                dve.wait_ge(biased, tile[0])
                w = P * (t + 1)
                step(dve.tensor_reduce(rs[:, u, 0, :, 1:3], sc[:, u, :, :, 0:w], AX, ALU.max, negate=True))
                step(dve.tensor_reduce(rs[:, u, 0, :, 0], sc_c[:, u, :, :], AX, ALU.max, negate=True))
                dve.tensor_scalar(rs[:, u, 0, :, 0], rs[:, u, 0, :, 0], 1.0e20, None, ALU.min).then_inc(max_ready, 1)

            def gated(a):
                p, g, t = ATT[a]
                u, w, G = a % 2, P * (t + 1), 2 * p + g
                dve.wait_ge(exp_done, a + 1)
                r = rs[:, u, 2, :, :]
                step(dve.tensor_scalar(r, rs[:, u, 1, :, :], 1.0e-30, None, ALU.max))
                step(dve.reciprocal(r, r))
                step(dve.tensor_tensor(r, r, gates[:, t, G * 12:(G + 1) * 12].rearrange("p (i b) -> p i b", i=HPG),
                                       ALU.mult))
                for i in range(HPG):
                    for br in range(2):
                        s = sc[:, u, i, br, 0:w]
                        ins = dve.tensor_scalar(s, s, rs[:, u, 2, i, 1 + br:2 + br], None, ALU.mult)
                s = sc_c[:, u, :, :]
                dve.tensor_tensor(s, s, rs[:, u, 2, :, 0:1].broadcast_to([P, HPG, 16]), ALU.mult).then_inc(p_ready, 1)

            biases(0)
            for a in range(len(ATT)):
                if a + 1 < len(ATT):
                    biases(a + 1)
                gated(a)
            dve.wait_ge(o_saved, len(ATT))
            dve.wait_ge(p_turned, turned[-1])
            heads = mix[:, 0:8, :].rearrange("p a b -> p (a b)")
            for c in range(4):
                o = heads[:, c * 512:(c + 1) * 512]
                dve.tensor_tensor(osq[:, c * 512:(c + 1) * 512], o, o, ALU.mult).then_inc(osq_ready, 1)
            dve.wait_ge(unit_saved, units_with("mo"))
            for h in range(ML_H):
                dve.wait_ge(num_done, h + 1)
                for t in range(TT):
                    dve.scalar_tensor_tensor(out=mo_v[:, t, h, :], in0=PS[:, 4 + h, t * P:(t + 1) * P],
                                             scalar=ml[:, 7, t, h:h + 1], in1=mo_v[:, t, h, :], op0=ALU.mult,
                                             op1=ALU.mult).then_inc(hm_ready, 1)
            dve.wait_ge(hm_ready, 2 * ML_H)
            sq = gmb[:, :, :, :].rearrange("p a b c -> p (a b c)")[:, 0:1024].rearrange("p (t h d) -> p t h d", t=TT,
                                                                                         h=ML_H)
            dve.wait_ge(s_turned, ML_H)
            step(dve.tensor_tensor(sq, mo_v, mo_v, ALU.mult))
            dve.tensor_reduce(ml[:, 10, :, :], sq, AX, ALU.add).then_inc(hm_sq, 1)
            for c in range(4):
                r = oroot_b[:, c * 512:(c + 1) * 512]
                o = heads[:, c * 512:(c + 1) * 512]
                dve.wait_ge(oroot, c + 1)
                step(dve.reciprocal(r, r))
                step(dve.tensor_tensor(o, o, r, ALU.mult))
                for k in (2 * c, 2 * c + 1):
                    dve.tensor_scalar(mix[:, k, :], mix[:, k, :], col("nsa_g", k), None, ALU.mult)\
                        .then_inc(attn_out, 1)
            dve.wait_ge(hm_root, 1)
            step(dve.reciprocal(ml[:, 11, :, :], ml[:, 11, :, :]))
            dve.tensor_tensor(mo_v, mo_v, ml[:, 11, :, :].unsqueeze(3).broadcast_to([P, TT, ML_H, P]), ALU.mult)\
                .then_inc(hm_norm, 1)
            dve.wait_ge(router_loaded, 16 * ROUTER_DMAS)
            dve.tensor_tensor(roww[:, :, :], roww[:, :, :],
                              ffn_gc[:, :, :].rearrange("p c j -> p (c j)").unsqueeze(2)
                              .broadcast_to([P, DK, EG + E]), ALU.mult).then_inc(roww_ready, 1)
            for v in range(4 * TT):
                m, t = v // TT, v % TT
                dve.wait_ge(out_done, v + 1)
                y = x1[:, t, m * 512:(m + 1) * 512]
                dve.tensor_tensor(y, PS[:, v, :], y, ALU.add).then_inc(out_added, 1)

            dve.wait_ge(ffn_ssq, 4 * TT)
            dve.tensor_reduce(st[:, 6:8], ssq[:, :, :], AX, ALU.add).then_inc(ffn_summed, 1)
            dve.wait_ge(gain_loaded, 16)
            dve.wait_ge(ffn_root, 1)
            step(dve.reciprocal(st[:, 8:10], st[:, 8:10]))
            for t in range(TT):
                for c in range(4):
                    ins = dve.scalar_tensor_tensor(
                        out=xn[:, t, 4 * c:4 * c + 4, :].rearrange("t j p -> t p j"),
                        in0=x1[:, t, c * 512:(c + 1) * 512].rearrange("t (p j) -> t p j", j=4),
                        scalar=st[:, 8 + t:9 + t],
                        in1=fin_g[:, c * 512:(c + 1) * 512].rearrange("t (p j) -> t p j", j=4),
                        op0=ALU.mult, op1=ALU.mult)
                ins.then_inc(xn_ready, 1)
            dve.memset(SW[:, 1, :], 0.0)
            dve.memset(Y2[:, 1, :], 0.0).then_inc(zeroed, 1)
            step(dve.memset(rank[:, :, E:], -1.0))
            step(dve.memset(wgt[:, :, E:], 0.0))

            dve.wait_ge(logits_done, 1)
            Lg, Le = ro[:, 8, :, 0:EG], ro[:, 1, :, :]
            for t in range(TT):
                for dst, c0, c1 in ((Lg, 0, EG), (Le, EG, EG + E)):
                    step(dve.scalar_tensor_tensor(out=dst[:, t, :], in0=PS[:, t, c0:c1], scalar=st[:, 8 + t:9 + t],
                                                  in1=rout_b[:, c0:c1], op0=ALU.mult, op1=ALU.add))

            def wide(v, n):
                return rt[:, v, :].unsqueeze(2).broadcast_to([P, TT, n])

            def pick(one, scores_, top, n, low):
                step(dve.tensor_reduce(rt[:, top, :], scores_, AX, ALU.max))
                step(dve.tensor_tensor(one, scores_, wide(top, n), ALU.is_equal))
                step(dve.tensor_tensor(one, one, low.unsqueeze(1).broadcast_to([P, TT, n]), ALU.mult))
                step(dve.tensor_reduce(rt[:, 15, :], one, AX, ALU.max))
                step(dve.tensor_tensor(one, one, wide(15, n), ALU.is_equal))

            og = ro[:, 9, :, 0:EG]
            pick(og, Lg, 0, EG, countdown[:, 0:EG])
            step(dve.tensor_tensor(ro[:, 6, :, 0:EG], Lg, wide(0, EG), ALU.subtract))
            step(dve.tensor_scalar(og, og, -NEG, NEG, ALU.mult, ALU.add))
            for t in range(TT):
                e4 = Le[:, t, :].rearrange("p (g e) -> p g e", g=EG)
                step(dve.tensor_tensor(e4, e4, og[:, t, :].unsqueeze(2).broadcast_to([P, EG, EI]), ALU.add))
            one1, one2, rest = ro[:, 2, :, :], ro[:, 3, :, :], ro[:, 4, :, :]
            pick(one1, Le, 1, E, countdown[:, :])
            step(dve.scalar_tensor_tensor(out=rest, in0=one1, scalar=3 * NEG, in1=Le, op0=ALU.mult, op1=ALU.add))
            pick(one2, rest, 2, E, countdown[:, :])
            dve.tensor_tensor(rt[:, 9, :], rt[:, 2, :], rt[:, 1, :], ALU.subtract).then_inc(route_max, 1)
            dve.wait_ge(route_exp, 2)
            step(dve.tensor_reduce(rt[:, 3, :], ro[:, 7, :, 0:EG], AX, ALU.add))
            step(dve.reciprocal(rt[:, 4, :], rt[:, 3, :]))
            step(dve.tensor_scalar(rt[:, 5, :], rt[:, 10, :], 1.0, None, ALU.add))
            step(dve.reciprocal(rt[:, 6, :], rt[:, 5, :]))
            step(dve.tensor_tensor(rt[:, 7, :], rt[:, 4, :], rt[:, 6, :], ALU.mult))
            step(dve.tensor_tensor(rt[:, 8, :], rt[:, 7, :], rt[:, 10, :], ALU.mult))
            A = ro[:, 0, :, :]
            dve.tensor_tensor(A, one1, one2, ALU.add).then_inc(picks_ready, 1)
            step(dve.tensor_tensor(ro[:, 5, :, :], one1, wide(7, E), ALU.mult))
            step(dve.tensor_tensor(ro[:, 10, :, :], one2, wide(8, E), ALU.mult))
            step(dve.tensor_tensor(wgt[:, :, 0:E], ro[:, 5, :, :], ro[:, 10, :, :], ALU.add))
            dve.wait_ge(ranks_done, 1)
            rk = PS[:, 5, 0:128].rearrange("p (t n) -> p t n", t=TT)[:, :, 0:E]
            step(dve.scalar_tensor_tensor(out=rank[:, :, 0:E], in0=rk, scalar=1.0, in1=A, op0=ALU.add, op1=ALU.mult))
            step(dve.tensor_scalar(rank[:, :, 0:E], rank[:, :, 0:E], -1.0, None, ALU.add))
            HT = PS[:, 1, :].rearrange("p (k n) -> p k n", k=4)

            def add_scattered(t, cols, done):
                y = x1[:, t, cols * 1024:(cols + 1) * 1024]
                dve.tensor_tensor(y, PS[:, 4:6, :].rearrange("p a b -> p (a b)"), y, ALU.add).then_inc(done, 1)

            def select(first, count):
                for t in range(TT):
                    dve.tensor_tensor(sel[:, t, :, :], slot_id[:, :].unsqueeze(1).broadcast_to([P, QUAD, SLOTS]),
                                      rank[:, t, bass.ds(first, QUAD)].unsqueeze(2).broadcast_to([P, QUAD, SLOTS]),
                                      ALU.is_equal).then_inc(sel_made, 1)
                dve.wait_ge(sel_made, count * TT + TT)
                for t in range(TT):
                    ins = dve.tensor_tensor(
                        selw[:, t, :, :], sel[:, t, :, :],
                        wgt[:, t, bass.ds(first, QUAD)].unsqueeze(2).broadcast_to([P, QUAD, SLOTS]), ALU.mult)
                ins.then_inc(sel_ready, 1)

            select(0, 0)
            made = [0]

            def listed(ins):
                made[0] += 1
                ins.then_inc(blocks_step, 1)
                dve.wait_ge(blocks_step, made[0])

            n_tok, more, first, end = (ovt[:, i:i + 1] for i in range(4))
            listed(dve.tensor_scalar(more, PS[0:E, 6, 0:1], float(SLOTS), None, ALU.is_gt))
            for r in (2, 3):
                listed(dve.scalar_tensor_tensor(out=more, in0=PS[0:E, 6, 0:1], scalar=float(r * SLOTS), in1=more,
                                                op0=ALU.is_gt, op1=ALU.add))
            dve.wait_ge(blocks_pe, 1)
            number = slot_id[0:E, 0:BLOCKS]
            listed(dve.tensor_copy(first, PS[0:E, 7, 0:1]))
            listed(dve.tensor_tensor(end, first, more, ALU.add))
            listed(dve.tensor_scalar(own[:, 0, :], number, first, None, ALU.is_ge))
            listed(dve.scalar_tensor_tensor(out=own[:, 2, :], in0=number, scalar=end, in1=own[:, 0, :],
                                            op0=ALU.is_lt, op1=ALU.mult))
            listed(dve.tensor_scalar(own[:, 1, :], number, first, 1.0, ALU.subtract, ALU.add))
            listed(dve.scalar_tensor_tensor(out=own[:, 1, :], in0=own[:, 1, :], scalar=float(SLOTS),
                                            in1=own[:, 2, :], op0=ALU.mult, op1=ALU.mult))
            listed(dve.tensor_scalar(own[:, 0, :], own[:, 2, :], row_id[:, :], None, ALU.mult))
            dve.wait_ge(blocks_pe, 2)
            dve.tensor_copy(blk_f[:, :], PS[:, 6, 64:64 + 3 * BLOCKS]).then_inc(blocks_ready, 1)
            dve.tensor_copy(blk_i[:, :], PS[0:1, 6, 64:64 + 3 * BLOCKS]).then_inc(blocks_ready, 1)
            dve.wait_ge(blocks_ready, 2)
            for counted in (y_saved_d, sc_added, hid_ready):
                dve.sem_inc(counted, 1)
            with dve.Fori(0, NQUAD) as q:
                for i in range(QUAD):
                    dve.wait_ge(sc_filled, q * 8 + (2 * i + 1))
                    add_scattered(i % 2, 0, sc_added)
                    dve.wait_ge(silu_done, q * QUAD + (i + 1))
                    dve.tensor_tensor(hTe[:, :, :], HT[:, :, SLOTS:2 * SLOTS], sg[:, :, :], ALU.mult)\
                        .then_inc(hid_ready, 1)
                    dve.wait_ge(sc_filled, q * 8 + (2 * i + 2))
                    add_scattered(i % 2, 1, sc_added)
                    dve.wait_ge(w_used[5], q * QUAD + (i + 1))
                    r = 64 * (i % 2)
                    dve.tensor_copy(Y2[r:r + 64, i // 2, 1024:2048],
                                    PS[64:128, 2:4, :].rearrange("p a b -> p (a b)")).then_inc(y_saved_d, 1)
                    if i == 2:
                        dve.wait_ge(sw_filled, q + 1)
                        select(q * QUAD + QUAD, q + 1)
            for t in range(TT):
                for cols in range(2):
                    dve.wait_ge(sc_filled, 8 * NQUAD + 2 * t + cols + 1)
                    add_scattered(t, cols, sc_added)
            dve.wait_ge(sc_added, 8 * NQUAD + 5)

            with dve.Fori(0, BLOCKS) as b:
                active = dve.value_load(blk_i[0:1, bass.ds(b + 2 * BLOCKS, 1)], min_val=0, max_val=1)
                e = dve.value_load(blk_i[0:1, bass.ds(b, 1)], min_val=0, max_val=E - 1)
                with dve.If(active > 0):
                    for t in range(TT):
                        dve.scalar_tensor_tensor(out=sel[:, t, 0, :], in0=slot_id[:, :],
                                                 scalar=blk_f[:, bass.ds(b + BLOCKS, 1)],
                                                 in1=rank[:, t, bass.ds(e, 1)].broadcast_to([P, SLOTS]),
                                                 op0=ALU.add, op1=ALU.is_equal).then_inc(ov_step, 1)
                    dve.wait_ge(ov_step, b * TT + TT)
                    for t in range(TT):
                        ins = dve.tensor_tensor(selw[:, t, 0, :], sel[:, t, 0, :],
                                                wgt[:, t, bass.ds(e, 1)].broadcast_to([P, SLOTS]), ALU.mult)
                    ins.then_inc(ov_sel, 1)
                    dve.wait_ge(ov_act, b * OV_ACT + 11)
                    dve.tensor_tensor(hTe[:, :, :], HT[:, :, SLOTS:2 * SLOTS], sg[:, :, :], ALU.mult)\
                        .then_inc(ov_dve, 1)
                    for i in range(4):
                        dve.wait_ge(ov_pe, b * OV_PE + (13 + i))
                        y = x1[:, i // 2, (i % 2) * 1024:(i % 2 + 1) * 1024]
                        dve.tensor_tensor(y, PS[:, OV_BANK[i]:OV_BANK[i] + 2, :].rearrange("p a b -> p (a b)"), y,
                                          ALU.add).then_inc(ov_dve, 1)
                    dve.wait_ge(ov_dve, b * OV_DVE + OV_DVE)
                    dve.sem_inc(ov_end, 1)
                with dve.Else():
                    dve.sem_inc(ov_dve, OV_DVE)
                    dve.sem_inc(ov_sel, 1)
                    dve.sem_inc(ov_step, TT)
                    dve.sem_inc(ov_end, 1)

            dve.wait_ge(fing_loaded, 16)
            dve.wait_ge(fin_root, 1)
            step(dve.reciprocal(st[:, 12:14], st[:, 12:14]))
            for t in range(TT):
                dve.scalar_tensor_tensor(out=x1[:, t, :], in0=x1[:, t, :], scalar=st[:, 12 + t:13 + t],
                                         in1=fin_g[:, :], op0=ALU.mult, op1=ALU.mult).then_inc(fin_ready, 1)


_INS = ['x', 'attn_norm_g', 'w_in', 'cmp_pos_k', 'cmp_w1_k', 'cmp_w2_k', 'cmp_pos_v', 'cmp_w1_v', 'cmp_w2_v',
        'nsa_out_g', 'mlstm_conv_w', 'mlstm_conv_b', 'mlstm_i_bias', 'mlstm_f_bias', 'mlstm_out_g', 'conv_w',
        'conv_b', 'conv_ln_g', 'conv_ln_b', 'w_out', 'ffn_norm_g', 'router_w_group', 'router_b_group',
        'router_w_expert', 'router_b_expert', 'expert_w_gate', 'expert_w_up', 'expert_w_down', 'final_norm_g']
_OUTS = [((1, T, D), 'float32')]


def kernel(**inputs):
    import numpy as _np
    import concourse.bacc as _bacc
    from concourse import mybir as _mybir
    from concourse.bass_utils import run_bass_kernel_spmd as _run

    nc = _bacc.Bacc("TRN2", target_bir_lowering=False, num_devices=1)
    arrays, args = {}, []
    for name in _INS:
        a = _np.ascontiguousarray(inputs[name])
        arrays[f"in_{name}_dram"] = a
        args.append(nc.dram_tensor(f"in_{name}_dram", a.shape, _mybir.dt.from_np(a.dtype), kind="ExternalInput").ap())
    for i, (shape, dtype) in enumerate(_OUTS):
        dt = _mybir.dt.from_np(_np.dtype(dtype))
        args.append(nc.dram_tensor(f"out_{i}_dram", shape, dt, kind="ExternalOutput").ap())
    build(nc, *args)
    r = _run(nc, [arrays], core_ids=[0])
    got = tuple(r.results[0][f"out_{i}_dram"] for i in range(len(_OUTS)))
    return got[0]
```
